# Optimizing a Trainium2 kernel written in Bass

```python
import math
import jax, jax.numpy as jnp
from jax import lax
import numpy as np

D_MODEL = 1024
BATCH = 1
SEQ = 256
DEPTH = 2

MIX_WIDTH = D_MODEL
N_MIXERS = 4
GROUP_WIDTH = MIX_WIDTH // N_MIXERS
BLOCK = 128
ROPE_THETA = 500000.0
NEG_INF = -1e30
EPS = 1e-6

DIFF_HEADS = 4
DIFF_DV = GROUP_WIDTH // DIFF_HEADS
DIFF_DK = DIFF_DV // 2
DIFF_ROPE = DIFF_DK // 4

MLA_HEADS = 4
MLA_NOPE = GROUP_WIDTH // MLA_HEADS
MLA_ROPE = MLA_NOPE // 2
MLA_V = GROUP_WIDTH // MLA_HEADS
MLA_Q_LORA = GROUP_WIDTH
MLA_KV_LORA = GROUP_WIDTH // 2

SGU_GROUPS = 4
SGU_CHUNK = 128
SGU_GROUP_DIM = GROUP_WIDTH // SGU_GROUPS

DIL_HEADS = 4
DIL_HD = GROUP_WIDTH // DIL_HEADS
DIL_ROPE = DIL_HD // 4
DIL_BRANCHES = ((128, 1), (512, 4), (2048, 16))

PEER_HEADS = 8
PEER_TOPK = 16
N_KEYS = 128
N_EXPERTS = N_KEYS * N_KEYS
PEER_DQ = 128
PEER_CHUNK = 128

A_QK = DIFF_HEADS * 2 * DIFF_DK
A_V = DIFF_HEADS * DIFF_DV
IN_SPLIT_SIZES = (A_QK, A_QK, A_V,
                  MLA_Q_LORA, MLA_KV_LORA, MLA_ROPE,
                  2 * GROUP_WIDTH,
                  GROUP_WIDTH, GROUP_WIDTH, GROUP_WIDTH)
IN_WIDTH = sum(IN_SPLIT_SIZES)

kernel_name = 'hybrid_parallel_heads_peer'

def _split_cols(z, sizes):
    out, start = [], 0
    for n in sizes:
        out.append(z[..., start:start + n])
        start += n
    return out

def _rmsnorm(x, g):
    xf = x.astype(jnp.float32)
    y = xf * lax.rsqrt(jnp.mean(xf * xf, axis=-1, keepdims=True) + EPS)
    return (y * g.astype(jnp.float32)).astype(x.dtype)

def _rope(x, n_rot):
    S = x.shape[1]
    half = n_rot // 2
    pos = jnp.arange(S, dtype=jnp.float32)
    inv = ROPE_THETA ** (-jnp.arange(half, dtype=jnp.float32) * (2.0 / n_rot))
    ang = pos[:, None] * inv[None, :]
    cos = jnp.cos(ang)[None, :, None, :]
    sin = jnp.sin(ang)[None, :, None, :]
    xf = x.astype(jnp.float32)
    x1 = xf[..., :half]
    x2 = xf[..., half:n_rot]
    out = jnp.concatenate([x1 * cos - x2 * sin, x2 * cos + x1 * sin, xf[..., n_rot:]], axis=-1)
    return out.astype(x.dtype)

def _to_blocks(a):
    B, S = a.shape[:2]
    return jnp.swapaxes(a.reshape(B, S // BLOCK, BLOCK, *a.shape[2:]), 0, 1)

def _from_blocks(a):
    nb, B = a.shape[:2]
    a = jnp.swapaxes(a, 0, 1)
    return a.reshape(B, nb * BLOCK, *a.shape[3:])

def _diff_attention(q, k, v, lam):
    S = q.shape[1]
    nb = S // BLOCK
    scale = DIFF_DK ** -0.5
    kpos = jnp.arange(S)

    def block(args):
        i, qi = args
        qpos = i * BLOCK + jnp.arange(BLOCK)
        s = jnp.einsum('bqhmd,bkhmd->bhmqk', qi, k).astype(jnp.float32) * scale
        s = jnp.where(kpos[None, :] <= qpos[:, None], s, NEG_INF)
        p = jax.nn.softmax(s, axis=-1)
        p = p[:, :, 0] - lam * p[:, :, 1]
        return jnp.einsum('bhqk,bkhd->bqhd', p.astype(v.dtype), v)

    o = lax.map(block, (jnp.arange(nb), _to_blocks(q)))
    return _from_blocks(o)

def _causal_attention(q, k, v, scale):
    S = q.shape[1]
    nb = S // BLOCK
    kpos = jnp.arange(S)

    def block(args):
        i, qi = args
        qpos = i * BLOCK + jnp.arange(BLOCK)
        s = jnp.einsum('bqhd,bkhd->bhqk', qi, k).astype(jnp.float32) * scale
        s = jnp.where(kpos[None, :] <= qpos[:, None], s, NEG_INF)
        p = jax.nn.softmax(s, axis=-1)
        return jnp.einsum('bhqk,bkhd->bqhd', p.astype(v.dtype), v)

    o = lax.map(block, (jnp.arange(nb), _to_blocks(q)))
    return _from_blocks(o)

def _spatial_gating(zc, v_norm, w_s, b_s):
    B, S, _ = zc.shape
    u, v = zc[..., :GROUP_WIDTH], zc[..., GROUP_WIDTH:]
    v = _rmsnorm(v, v_norm)
    v = v.reshape(B, S // SGU_CHUNK, SGU_CHUNK, SGU_GROUPS, SGU_GROUP_DIM)
    w = w_s * jnp.tril(jnp.ones((SGU_CHUNK, SGU_CHUNK), w_s.dtype))
    sv = jnp.einsum('gts,bcsge->bctge', w, v) + b_s.T[:, :, None]
    return u * sv.reshape(B, S, GROUP_WIDTH)

def _dilated_attention(q, k, v):
    S = q.shape[1]
    nb = S // BLOCK
    scale = DIL_HD ** -0.5

    def block(args):
        i, qi = args
        qpos = i * BLOCK + jnp.arange(BLOCK)
        outs, lses = [], []
        for window, dil in DIL_BRANCHES:
            n = window // dil + 1
            idx = qpos[:, None] - dil * jnp.arange(n)[None, :]
            valid = idx >= 0
            idx = jnp.maximum(idx, 0)
            kg = k[:, idx]
            vg = v[:, idx]
            s = jnp.einsum('bqhe,bqjhe->bqhj', qi, kg).astype(jnp.float32) * scale
            s = jnp.where(valid[None, :, None, :], s, NEG_INF)
            m = jnp.max(s, axis=-1, keepdims=True)
            e = jnp.exp(s - m)
            den = jnp.sum(e, axis=-1, keepdims=True)
            outs.append(jnp.einsum('bqhj,bqjhe->bqhe', (e / den).astype(v.dtype), vg))
            lses.append((m + jnp.log(den))[..., 0])
        wts = jax.nn.softmax(jnp.stack(lses, axis=0), axis=0)
        o = jnp.sum(wts[..., None] * jnp.stack(outs, axis=0).astype(jnp.float32), axis=0)
        return o.astype(v.dtype)

    o = lax.map(block, (jnp.arange(nb), _to_blocks(q)))
    return _from_blocks(o)

def _peer(h, w_q, sub_keys, exp_u, exp_v):
    B, S, D = h.shape
    T = B * S
    half = PEER_DQ // 2
    hc = h.reshape(T // PEER_CHUNK, PEER_CHUNK, D)

    def chunk(xc):
        q = (xc @ w_q).reshape(PEER_CHUNK, PEER_HEADS, 2, half)
        s = jnp.einsum('thce,cne->thcn', q, sub_keys).astype(jnp.float32)
        sv, si = lax.top_k(s, PEER_TOPK)
        cand = (sv[:, :, 0, :, None] + sv[:, :, 1, None, :]).reshape(PEER_CHUNK, PEER_HEADS, PEER_TOPK * PEER_TOPK)
        cidx = (si[:, :, 0, :, None] * N_KEYS + si[:, :, 1, None, :]).reshape(PEER_CHUNK, PEER_HEADS, PEER_TOPK * PEER_TOPK)
        top, pos = lax.top_k(cand, PEER_TOPK)
        eidx = jnp.take_along_axis(cidx, pos, axis=-1)
        g = jax.nn.softmax(top, axis=-1)
        a = jax.nn.gelu(jnp.einsum('td,thkd->thk', xc, exp_u[eidx]).astype(jnp.float32))
        return jnp.einsum('thk,thkd->td', (g * a).astype(exp_v.dtype), exp_v[eidx])

    return lax.map(chunk, hc).reshape(B, S, D)

def setup_inputs(seed: int = 0) -> dict:
    key = jax.random.key(seed)
    ks = jax.random.split(key, 24)

    def nrm(k, shape, scale):
        return jax.random.normal(k, shape, jnp.float32) * scale

    def gain(k, shape):
        return 1.0 + 0.02 * jax.random.normal(k, shape, jnp.float32)

    L = DEPTH
    return {
        'x': nrm(ks[0], (BATCH, SEQ, D_MODEL), 1.0),
        'w_in': nrm(ks[1], (L, D_MODEL, IN_WIDTH), D_MODEL ** -0.5),
        'w_out': nrm(ks[2], (L, MIX_WIDTH, D_MODEL), MIX_WIDTH ** -0.5),
        'norm_mix': gain(ks[3], (L, D_MODEL)),
        'norm_ffn': gain(ks[4], (L, D_MODEL)),
        'diff_lambda': nrm(ks[5], (L, 4, DIFF_DK), 0.1),
        'diff_head_norm': gain(ks[6], (L, A_V)),
        'mla_q_norm': gain(ks[7], (L, MLA_Q_LORA)),
        'mla_kv_norm': gain(ks[8], (L, MLA_KV_LORA)),
        'mla_w_uq': nrm(ks[9], (L, MLA_Q_LORA, MLA_HEADS * (MLA_NOPE + MLA_ROPE)), MLA_Q_LORA ** -0.5),
        'mla_w_ukv': nrm(ks[10], (L, MLA_KV_LORA, MLA_HEADS * (MLA_NOPE + MLA_V)), MLA_KV_LORA ** -0.5),
        'mla_out_norm': gain(ks[11], (L, GROUP_WIDTH)),
        'sgu_v_norm': gain(ks[12], (L, GROUP_WIDTH)),
        'sgu_w': nrm(ks[13], (L, SGU_GROUPS, SGU_CHUNK, SGU_CHUNK), SGU_CHUNK ** -0.5),
        'sgu_b': gain(ks[14], (L, SGU_GROUPS, SGU_CHUNK)),
        'sgu_out_norm': gain(ks[15], (L, GROUP_WIDTH)),
        'dil_out_norm': gain(ks[16], (L, GROUP_WIDTH)),
        'peer_w_q': nrm(ks[17], (L, D_MODEL, PEER_HEADS * PEER_DQ), D_MODEL ** -0.5),
        'peer_sub_keys': nrm(ks[18], (L, 2, N_KEYS, PEER_DQ // 2), (PEER_DQ // 2) ** -0.5),
        'peer_u': nrm(ks[19], (L, N_EXPERTS, D_MODEL), D_MODEL ** -0.5),
        'peer_v': nrm(ks[20], (L, N_EXPERTS, D_MODEL), PEER_HEADS ** -0.5),
        'final_norm': gain(ks[21], (D_MODEL,)),
    }

def reference(x, w_in, w_out, norm_mix, norm_ffn, diff_lambda, diff_head_norm,
              mla_q_norm, mla_kv_norm, mla_w_uq, mla_w_ukv, mla_out_norm,
              sgu_v_norm, sgu_w, sgu_b, sgu_out_norm, dil_out_norm,
              peer_w_q, peer_sub_keys, peer_u, peer_v, final_norm):
    B, S, _ = x.shape
    for l in range(DEPTH):
        h = _rmsnorm(x, norm_mix[l])
        z = h @ w_in[l]
        aq, ak, av, cq, ckv, kpe, zc, dq, dk, dv = _split_cols(z, IN_SPLIT_SIZES)

        lam_init = 0.8 - 0.6 * math.exp(-0.3 * l)
        lf = diff_lambda[l].astype(jnp.float32)
        lam = jnp.exp(jnp.sum(lf[0] * lf[1])) - jnp.exp(jnp.sum(lf[2] * lf[3])) + lam_init
        aq = _rope(aq.reshape(B, S, DIFF_HEADS * 2, DIFF_DK), DIFF_ROPE).reshape(B, S, DIFF_HEADS, 2, DIFF_DK)
        ak = _rope(ak.reshape(B, S, DIFF_HEADS * 2, DIFF_DK), DIFF_ROPE).reshape(B, S, DIFF_HEADS, 2, DIFF_DK)
        oa = _diff_attention(aq, ak, av.reshape(B, S, DIFF_HEADS, DIFF_DV), lam)
        oa = (_rmsnorm(oa, diff_head_norm[l].reshape(DIFF_HEADS, DIFF_DV)) * (1.0 - lam_init)).reshape(B, S, GROUP_WIDTH)

        cq = _rmsnorm(cq, mla_q_norm[l])
        ckv = _rmsnorm(ckv, mla_kv_norm[l])
        q = (cq @ mla_w_uq[l]).reshape(B, S, MLA_HEADS, MLA_NOPE + MLA_ROPE)
        q = jnp.concatenate([q[..., :MLA_NOPE], _rope(q[..., MLA_NOPE:], MLA_ROPE)], axis=-1)
        kv = (ckv @ mla_w_ukv[l]).reshape(B, S, MLA_HEADS, MLA_NOPE + MLA_V)
        k_pe = jnp.broadcast_to(_rope(kpe[:, :, None, :], MLA_ROPE), (B, S, MLA_HEADS, MLA_ROPE))
        k = jnp.concatenate([kv[..., :MLA_NOPE], k_pe], axis=-1)
        ob = _causal_attention(q, k, kv[..., MLA_NOPE:], (MLA_NOPE + MLA_ROPE) ** -0.5)
        ob = _rmsnorm(ob.reshape(B, S, GROUP_WIDTH), mla_out_norm[l])

        oc = _spatial_gating(jax.nn.gelu(zc), sgu_v_norm[l], sgu_w[l], sgu_b[l])
        oc = _rmsnorm(oc, sgu_out_norm[l])

        dq = _rope(dq.reshape(B, S, DIL_HEADS, DIL_HD), DIL_ROPE)
        dk = _rope(dk.reshape(B, S, DIL_HEADS, DIL_HD), DIL_ROPE)
        od = _dilated_attention(dq, dk, dv.reshape(B, S, DIL_HEADS, DIL_HD))
        od = _rmsnorm(od.reshape(B, S, GROUP_WIDTH), dil_out_norm[l])

        x = x + jnp.concatenate([oa, ob, oc, od], axis=-1) @ w_out[l]

        x = x + _peer(_rmsnorm(x, norm_ffn[l]), peer_w_q[l], peer_sub_keys[l], peer_u[l], peer_v[l])
    return _rmsnorm(x, final_norm)


_drawn_inputs = setup_inputs


def setup_inputs(seed=0):
    import zlib

    import numpy as np

    out = dict(_drawn_inputs(seed))
    spreads = {}
    factors = {'diff_head_norm': 36.256,
     'mla_q_norm': 3.21,
     'mla_out_norm': 29.964,
     'sgu_v_norm': 100.371,
     'sgu_b': 72.81,
     'sgu_out_norm': 30.063,
     'dil_out_norm': 28.299,
     'final_norm': 20.578,
     'norm_ffn': 15.313}
    for name, (base, spread) in spreads.items():
        noise = np.random.default_rng([zlib.crc32(name.encode()), seed]).standard_normal(out[name].shape)
        drawn = base * np.exp(spread * noise) if base else spread * noise
        out[name] = __import__('jax').numpy.asarray(drawn.astype(out[name].dtype))
    for name, factor in factors.items():
        out[name] = (out[name] * factor).astype(out[name].dtype)
    return out
```

```python
import math
from contextlib import ExitStack

import numpy as np
import concourse.bass as bass
from concourse import mybir


def bass_hybrid_trunk_peer(
    nc: bass.Bass,
    x_in: bass.AP,
    w_in: bass.AP,
    w_out: bass.AP,
    w_q: bass.AP,
    columns: bass.AP,
    rows: bass.AP,
    layer_consts: bass.AP,
    w_uq: bass.AP,
    w_ukv: bass.AP,
    sgu_wt: bass.AP,
    keys_t: bass.AP,
    experts_u: bass.AP,
    experts_v: bass.AP,
    final_gain: bass.AP,
    masks: bass.AP,
    rope: bass.AP,
    triangle: bass.AP,
    identity: bass.AP,
    out: bass.AP,
):
    fp32 = mybir.dt.float32
    u32 = mybir.dt.uint32
    ALU = mybir.AluOpType
    ACT = mybir.ActivationFunctionType
    AX = mybir.AxisListType.X

    P = 128
    L = w_in.shape[0]
    D = x_in.shape[1]
    T = x_in.shape[0] // P
    S = x_in.shape[0]
    KC = D // P
    IN_W = w_in.shape[2]
    CH = 512
    EPS = 1e-6
    GROUP = D // 4
    Z_AQ, Z_AV, Z_CQ, Z_KPE, Z_U, Z_V, Z_DQ, Z_DV = 0, 512, 768, 1152, 1184, 1440, 1696, 2208
    C_MIX, C_QKV, C_OUT, C_SGUB, NCOL = 0, 8, 11, 19, 23
    R_SGU, R_FFN, R_LAM, NROW = 0, GROUP, GROUP + D, GROUP + D + 128
    HEADS = 4
    MQ = 96
    PH, TOPK, NKEY = 8, 16, 128
    PICKS = PH * TOPK
    SLOTS = 8
    GROUPS = PICKS // SLOTS
    W_SLOTS = 3
    LOWEST = -3.0e38

    UNITS = [(g, t) for g in ("diff", "dil", "mla") for t in range(T)]
    MAPS = {"diff": 8, "dil": 4, "mla": 4}
    SCALE = {"diff": 32 ** -0.5, "dil": 64 ** -0.5, "mla": MQ ** -0.5}
    MIX_AT = {"diff": 0, "mla": GROUP, "dil": 3 * GROUP}

    def keys(t):
        return P * (t + 1)

    ROW_TILES = {"diff": 4, "dil": 2, "mla": 1}

    def score_maps(u):
        g, t = UNITS[u]
        r, per = ROW_TILES[g], min(MAPS[g] // ROW_TILES[g], CH // keys(t))
        return [list(range(i + n * per * r, MAPS[g], r))[:per] for n in range(MAPS[g] // r // per) for i in range(r)]

    def score_jobs(u):
        return len(score_maps(u))

    def turn_jobs(u):
        return HEADS * (UNITS[u][1] + 1) // 4

    def unit_scores(u):
        return [("scores", u, n) for n in range(score_jobs(u))]

    V_JOBS = [("hT", t, j) for t in range(T) for j in range(2)]
    V_JOBS += [("qkT", "diff", t) for t in range(T)]
    V_JOBS += unit_scores(0) + unit_scores(1)
    V_JOBS += [("cT", t) for t in range(T)]
    V_JOBS += [("qkT", "dil", t) for t in range(T)]
    V_JOBS += [("pv", 0)] + unit_scores(2) + [("pv", 1)] + unit_scores(3)
    V_JOBS += [("qkT", "mla", t, j) for t in range(T) for j in range(2)]
    V_JOBS += [("pv", 2)] + unit_scores(4) + [("pv", 3)] + unit_scores(5)
    V_JOBS += [("sgu", t) for t in range(T)]
    V_JOBS += [("pv", 4), ("pv", 5)]
    V_JOBS += [("mixT", t, j) for t in range(T) for j in range(2)]
    V_JOBS += [("proj", c, t) for c in range(2) for t in range(T)]

    S_JOBS = [("z", c, t) for c in range(5) for t in range(T)]
    S_JOBS += [("mq", t) for t in range(T)] + [("mkv", t) for t in range(T)]
    S_JOBS += [("turn", u, n) for u in range(len(UNITS)) for n in range(turn_jobs(u))]
    S_JOBS += [("h2T", t, j) for t in range(T) for j in range(2)]
    S_JOBS += [("peerq", j) for j in range(4)]
    S_JOBS += [("keys", t, j) for t in range(T) for j in range(4)]
    V_AT = {job: n for n, job in enumerate(V_JOBS)}
    S_AT = {job: n for n, job in enumerate(S_JOBS)}

    POWERS = {"mix_in": (0, 2), "latent": (2, 4), "gate": (6, 2), "mixed": (8, 14), "ffn": (22, 2), "final": (24, 2)}
    POWER_AT = {name: n for n, name in enumerate(POWERS)}

    ctx = ExitStack()
    with ctx:
        def sb(name, shape, dt=fp32):
            return ctx.enter_context(nc.sbuf_tensor(name, shape, dt))

        taken = []

        def sem(name):
            s = ctx.enter_context(nc.semaphore(name))
            taken.append(s)
            return s

        x = sb("x", [P, T, D])
        wide = sb("wide", [P, T, D])
        hT = sb("hT", [P, KC, S])
        z = sb("z", [P, T, IN_W])
        ring = sb("ring", [P, W_SLOTS, KC, CH])
        gathered = sb("gathered", [P, SLOTS, D])
        scores = sb("scores", [P, 2, 8 * 256])
        probsT = sb("probsT", [P, HEADS, T, P])
        qkT = {"diff": sb("qkT_diff", [P, 4, S]), "dil": sb("qkT_dil", [P, 4, S]), "mla": sb("qkT_mla", [P, 8, S])}
        peer_qT = qkT["mla"]
        mq = sb("mq", [P, T, HEADS, MQ])
        mk = sb("mk", [P, T, HEADS, MQ])
        mv = sb("mv", [P, T, HEADS, 64])
        cn = sb("cn", [P, T, 3 * P])
        cT = sb("cT", [P, 3, S])
        uq_sb = sb("uq_sb", [P, 2, HEADS * MQ])
        ukv_sb = sb("ukv_sb", [P, 512])
        sgu_sb = sb("sgu_sb", [P, 4, P])
        keys_sb = sb("keys_sb", [P, NKEY])
        col = sb("col", [P, NCOL])
        row = sb("row", [P, NROW])
        lay = sb("lay", [P, 3])
        mask_sb = sb("mask_sb", [P, 2, T, 256])
        rope_sb = sb("rope_sb", [P, 2, T, 28])
        tri_sb = sb("tri_sb", [P, P])
        id_sb = sb("id_sb", [P, P])
        iota16 = sb("iota16", [P, TOPK])
        iota16_i = sb("iota16_i", [P, TOPK], mybir.dt.int32)
        half_neg = sb("half_neg", [P, 16])
        ms = sb("ms", [P, 26])
        rstd = sb("rstd", [P, 26])
        sumsq = sb("sumsq", [P, 44])
        rot = sb("rot", [P, 4, 256])
        neg_max = sb("neg_max", [P, 2, 8])
        den = sb("den", [P, 2, 8])
        rden = sb("rden", [P, 2, 8])
        lam_prod = sb("lam_prod", [P, 2, 32])
        lam_sum = sb("lam_sum", [P, 2])
        lam_exp = sb("lam_exp", [P, 2])
        lam = sb("lam", [P, 1])
        top_i = sb("top_i", [P, 2 * PH, TOPK], u32)
        best = sb("best", [P, T, PH, TOPK])
        pos = sb("pos", [P, PH, TOPK], u32)
        pos_hi = sb("pos_hi", [P, PH, TOPK], u32)
        pos_hi_f = sb("pos_hi_f", [P, PH, TOPK])
        pos_f = sb("pos_f", [P, PH, TOPK])
        key_of = sb("key_of", [P, 2, PH, TOPK])
        expert_f = sb("expert_f", [P, PICKS])
        expert = sb("expert", [P, T, PICKS], u32)
        index_slot = sb("index_slot", [P, SLOTS], u32)
        gate = sb("gate", [P, T, PH, TOPK])
        gate_sum = sb("gate_sum", [P, PH])
        dots = sb("dots", [P, T, PICKS])
        act_dots = sb("act_dots", [P, T, PICKS])
        key_scores = z[:, :, 0:2 * PH * NKEY].rearrange("p t (h n) -> p t h n", n=NKEY)
        pairs = scores[:, 0, :].rearrange("p (h i j) -> p h i j", i=TOPK, j=TOPK)
        onehot = scores[:, 1, :].rearrange("p (h k i) -> p h k i", k=TOPK, i=TOPK)
        flat_cn = cn[:, :, :].rearrange("p t n -> p (t n)")
        top_v = flat_cn[:, 0:2 * PH * TOPK].rearrange("p (h k) -> p h k", k=TOPK)
        top_f = flat_cn[:, 2 * PH * TOPK:4 * PH * TOPK].rearrange("p (h k) -> p h k", k=TOPK)
        mix = wide

        v_bank = [ctx.enter_context(nc.psum_tensor(f"v_bank{i}", [P, CH], fp32)) for i in range(4)]
        s_bank = [ctx.enter_context(nc.psum_tensor(f"s_bank{i}", [P, CH], fp32)) for i in range(4)]

        const_loaded = ctx.enter_context(nc.semaphore("const_loaded"))
        const_made = ctx.enter_context(nc.semaphore("const_made"))
        stored = ctx.enter_context(nc.semaphore("stored"))
        row_loaded = [ctx.enter_context(nc.semaphore(f"row_loaded{i}")) for i in range(SLOTS)]
        small_loaded = sem("small_loaded")
        chunk_loaded = [sem(f"chunk_loaded{i}") for i in range(W_SLOTS)]
        v_filled, v_emptied = sem("v_filled"), sem("v_emptied")
        s_filled, s_emptied = sem("s_filled"), sem("s_emptied")
        squared = sem("squared")
        ms_ready = sem("ms_ready")
        rstd_ready = sem("rstd_ready")
        vector_step = sem("vector_step")
        gpsimd_step = sem("gpsimd_step")
        scalar_step = sem("scalar_step")
        h_ready = sem("h_ready")
        latents_ready = sem("latents_ready")
        lam_summed = sem("lam_summed")
        lam_exped = sem("lam_exped")
        gated = sem("gated")
        gate_normed = sem("gate_normed")
        rotated = {g: sem(f"rotated_{g}") for g in ("diff", "dil", "mla")}
        sgu_masked = sem("sgu_masked")
        masked = sem("masked")
        exped = sem("exped")
        combined = sem("combined")
        mix_squared = sem("mix_squared")
        mix_ready = sem("mix_ready")
        mix_done = sem("mix_done")
        x_ready = sem("x_ready")
        h2_ready = sem("h2_ready")
        experts_ready = sem("experts_ready")
        shifted = sem("shifted")
        gates_exped = sem("gates_exped")
        index_copied = sem("index_copied")
        gather_turn = sem("gather_turn")
        slots_free = sem("slots_free")
        dots_done = sem("dots_done")
        dots_gelud = sem("dots_gelud")

        def bc(ap, axis, n):
            a = ap.unsqueeze(axis)
            shape = list(a.shape)
            shape[axis] = n
            return a.to_broadcast(shape)

        class Counted:

            def __init__(self, eng):
                self.eng, self.value = eng, {}

            def go(self, ins, s, n=1):
                ins.then_inc(s, n)
                self.value[id(s)] = self.value.get(id(s), 0) + n

            def link(self, ins, s):
                self.go(ins, s)
                self.eng.wait_ge(s, self.value[id(s)])

        def unit_view(u):
            g, t = UNITS[u]
            n = MAPS[g]
            return scores[:, u % 2, 0:n * keys(t)].rearrange("p (m k) -> p m k", m=n)

        with nc.Block() as block:
            @block.sync
            def _(sp):
                sp.dma_start(x[:, :, :], x_in.rearrange("(t p) d -> p t d", p=P)).then_inc(const_loaded, 16)
                sp.dma_start(mask_sb[:, :, :, :], masks).then_inc(const_loaded, 16)
                sp.dma_start(rope_sb[:, :, :, :], rope).then_inc(const_loaded, 16)
                sp.dma_start(tri_sb[:, :], triangle).then_inc(const_loaded, 16)
                sp.dma_start(id_sb[:, :], identity).then_inc(const_loaded, 16)
                sp.wait_ge(const_loaded, 5 * 16)

            @block.gpsimd
            def _(pool):
                nc.gpsimd.memset(half_neg[:, :], -0.5).then_inc(const_made, 1)
                nc.gpsimd.iota(iota16_i[:, :], [[1, TOPK]], base=0, channel_multiplier=0).then_inc(const_made, 1)
                pool.wait_ge(const_made, 2)
                nc.gpsimd.tensor_copy(iota16[:, :], iota16_i[:, :]).then_inc(const_made, 1)
                pool.wait_ge(const_made, 3)

        with nc.Fori(0, L) as layer:
            with nc.Block() as block:

                @block.sync
                def _(sp):
                    last_use = [("s", ("z", c, T - 1)) for c in range(5)]
                    last_use += [("v", ("proj", c, T - 1)) for c in range(2)]
                    for c in range(9):
                        if c >= W_SLOTS:
                            side, job = last_use[c - W_SLOTS]
                            if side == "s":
                                sp.wait_ge(s_filled, S_AT[job] + 1)
                            else:
                                sp.wait_ge(v_filled, V_AT[job] + 1)
                        w, at = (w_in, c * CH) if c < 5 else (w_out, (c - 5) * CH) if c < 7 else (w_q, (c - 7) * CH)
                        n = min(CH, w.shape[2] - at)
                        src = w[bass.ds(layer, 1)].rearrange("o (k p) n -> p (o k) n", p=P)[:, :, at:at + n]
                        sp.dma_start(ring[:, c % W_SLOTS, :, 0:n], src).then_inc(chunk_loaded[c % W_SLOTS], 16)

                @block.scalar
                def _(act):
                    own = Counted(act)
                    taken_jobs = []

                    def take(*job):
                        n = len(taken_jobs)
                        assert S_JOBS[n] == job, (S_JOBS[n], job)
                        taken_jobs.append(job)
                        act.wait_ge(s_filled, n + 1)
                        return s_bank[n % 4]

                    one = bass.ds(layer, 1)
                    act.dma_start(col[:, :], columns[one].rearrange("o p n -> p (o n)")).then_inc(small_loaded, 16)
                    act.dma_start(row[:, :], rows[one].to_broadcast([P, NROW])).then_inc(small_loaded, 16)
                    act.dma_start(lay[:, :], layer_consts[one].rearrange("o p n -> p (o n)")).then_inc(small_loaded, 16)
                    act.dma_start(uq_sb[:, :, :], w_uq[one].rearrange("o (k p) n -> p (o k) n", p=P)).then_inc(small_loaded, 16)
                    act.dma_start(ukv_sb[:, :], w_ukv[one].rearrange("o p n -> p (o n)")).then_inc(small_loaded, 16)
                    act.dma_start(sgu_sb[:, :, :], sgu_wt[one].rearrange("o s g t -> s (o g) t")).then_inc(small_loaded, 16)
                    act.dma_start(keys_sb[:, :], keys_t[one].rearrange("o p n -> p (o n)")).then_inc(small_loaded, 16)

                    for t in range(T):
                        own.go(nc.scalar.activation(gathered[:, t, :], x[:, t, :], ACT.Square,
                                                    accum_out=sumsq[:, t:t + 1]), squared)
                    act.wait_ge(lam_summed, 1)
                    own.link(nc.scalar.activation(lam_exp[:, :], lam_sum[:, :], ACT.Exp), lam_exped)
                    for c in range(5):
                        n = min(CH, IN_W - c * CH)
                        for t in range(T):
                            bank = take("z", c, t)
                            own.go(nc.scalar.activation(z[:, t, c * CH:c * CH + n], bank[:, 0:n], ACT.Copy), s_emptied)
                        if c == 2:
                            act.wait_ge(s_emptied, S_AT["z", 2, T - 1] + 1)
                            for t in range(T):
                                for j, (at, w) in enumerate(((Z_CQ, 256), (Z_CQ + 256, 128))):
                                    own.go(nc.scalar.activation(cn[:, t, 256 * j:256 * j + w], z[:, t, at:at + w],
                                                                ACT.Square, accum_out=sumsq[:, 2 + 2 * t + j:3 + 2 * t + j]), squared)
                    act.wait_ge(s_emptied, S_AT["z", 3, T - 1] + 1)
                    for t in range(T):
                        own.link(nc.scalar.activation(z[:, t, Z_U:Z_U + 512], z[:, t, Z_U:Z_U + 512],
                                                      ACT.Gelu_apprx_tanh), gated)
                    for t in range(T):
                        own.go(nc.scalar.activation(gathered[:, 2 + t, 0:GROUP], z[:, t, Z_V:Z_V + 256], ACT.Square,
                                                    accum_out=sumsq[:, 6 + t:7 + t]), squared)

                    def exps(u):
                        g, t = UNITS[u]
                        act.wait_ge(masked, u + 1)
                        s = unit_view(u)
                        for m in range(MAPS[g]):
                            ins = nc.scalar.activation(s[:, m, :], s[:, m, :], ACT.Exp, bias=neg_max[:, u % 2, m:m + 1],
                                                       accum_out=den[:, u % 2, m:m + 1])
                            own.go(ins, exped)

                    def turned(u):
                        g, t = UNITS[u]
                        flat = probsT[:, :, 0:t + 1, :]
                        for n in range(turn_jobs(u)):
                            bank = take("turn", u, n)
                            h0, hn = n * 4 // (t + 1), 4 // (t + 1)
                            own.go(nc.scalar.activation(
                                flat[:, h0:h0 + hn, :, :],
                                bank[:, :].rearrange("p (h k q) -> p h k q", h=hn, k=t + 1), ACT.Copy), s_emptied)

                    exps(0)
                    exps(1)
                    for t in range(T):
                        bank = take("mq", t)
                        own.go(nc.scalar.activation(mq[:, t, :, :].rearrange("p h e -> p (h e)"),
                                                    bank[:, 0:HEADS * MQ], ACT.Copy), s_emptied)
                    for t in range(T):
                        bank = take("mkv", t)[:, :].rearrange("p (h e) -> p h e", h=HEADS)
                        own.go(nc.scalar.activation(mk[:, t, :, 0:64], bank[:, :, 0:64], ACT.Copy), scalar_step)
                        own.go(nc.scalar.activation(mv[:, t, :, :], bank[:, :, 64:128], ACT.Copy), s_emptied)
                    for u in range(4):
                        turned(u)
                        exps(u + 2)
                    turned(4)
                    turned(5)

                    for t in range(T):
                        act.wait_ge(mix_done, t + 1)
                        act.wait_ge(s_filled, S_AT["turn", 4 + t, turn_jobs(4 + t) - 1] + 1)
                        own.go(nc.scalar.activation(scores[:, t, 0:D], mix[:, t, :], ACT.Square), mix_squared)
                    for t in range(T):
                        act.wait_ge(x_ready, t + 1)
                        own.go(nc.scalar.activation(gathered[:, 4 + t, :], x[:, t, :], ACT.Square,
                                                    accum_out=sumsq[:, 8 + t:9 + t]), squared)
                    for t in range(T):
                        for j in range(2):
                            bank = take("h2T", t, j)
                            own.go(nc.scalar.activation(hT[:, 4 * j:4 * j + 4, t * P:(t + 1) * P],
                                                        bank[:, :].rearrange("p (k q) -> p k q", k=4), ACT.Copy), s_emptied)
                    for j in range(4):
                        bank = take("peerq", j)
                        own.go(nc.scalar.activation(peer_qT[:, 2 * j:2 * j + 2, :],
                                                    bank[:, :].rearrange("p (h q) -> p h q", h=2), ACT.Copy), s_emptied)
                    for t in range(T):
                        for j in range(4):
                            bank = take("keys", t, j)
                            by_half = key_scores[:, t, :, :].rearrange("p (h c) n -> p h c n", c=2)
                            h0 = j // 2 * 4
                            own.go(nc.scalar.activation(by_half[:, h0:h0 + 4, j % 2, :],
                                                        bank[:, :].rearrange("p (h n) -> p h n", h=4), ACT.Copy), s_emptied)
                    for t in range(T):
                        act.wait_ge(shifted, t + 1)
                        own.go(nc.scalar.activation(gate[:, t, :, :], gate[:, t, :, :], ACT.Exp), gates_exped)
                    for t in range(T):
                        act.wait_ge(dots_done, t + 1)
                        own.go(nc.scalar.activation(act_dots[:, t, :], dots[:, t, :], ACT.Gelu_apprx_tanh), dots_gelud)

                @block.tensor
                def _(pe):
                    counts = {"v": 0, "s": 0}

                    def fill(side, *job):
                        n = counts[side]
                        jobs, emptied, bank = (V_JOBS, v_emptied, v_bank) if side == "v" else (S_JOBS, s_emptied, s_bank)
                        assert jobs[n] == job, (jobs[n], job)
                        counts[side] += 1
                        if n >= 4:
                            pe.wait_ge(emptied, n - 3)
                        return bank[n % 4]

                    def v_done(*job):
                        pe.wait_ge(v_emptied, V_AT[job] + 1)

                    def s_done(*job):
                        pe.wait_ge(s_emptied, S_AT[job] + 1)

                    def transposes(bank, blocks, rows_out=P):
                        for n, b in enumerate(blocks):
                            last = nc.tensor.transpose(bank[0:rows_out, n * P:(n + 1) * P], b, id_sb[:, :])
                        return last

                    for t in range(T):
                        pe.wait_ge(h_ready, t + 1)
                        for j in range(2):
                            bank = fill("v", "hT", t, j)
                            transposes(bank, [wide[:, t, k * P:(k + 1) * P] for k in range(4 * j, 4 * j + 4)]).then_inc(v_filled, 1)
                    for c in range(5):
                        n = min(CH, IN_W - c * CH)
                        pe.wait_ge(chunk_loaded[c % W_SLOTS], 16 * (c // W_SLOTS + 1))
                        for t in range(T):
                            bank = fill("s", "z", c, t)
                            v_done("hT", t, 1)
                            for k in range(KC):
                                last = nc.tensor.matmul(bank[:, 0:n], hT[:, k, t * P:(t + 1) * P],
                                                        ring[:, c % W_SLOTS, k, 0:n], start=(k == 0), stop=(k == KC - 1))
                            last.then_inc(s_filled, 1)

                    def turn_heads(g, at):
                        pe.wait_ge(rotated[g], 1)
                        for t in range(T):
                            bank = fill("v", "qkT", g, t)
                            transposes(bank, [z[:, t, at + b * P:at + (b + 1) * P] for b in range(4)]).then_inc(v_filled, 1)

                    def head_views(g, t, m):
                        kk, q = slice(0, keys(t)), slice(t * P, (t + 1) * P)
                        if g == "mla":
                            return qkT[g][0:MQ, m, q], qkT[g][0:MQ, 4 + m, kk]
                        w = 32 if g == "diff" else 64
                        per = P // w
                        rows_ = slice(w * (m % per), w * (m % per) + w)
                        return qkT[g][rows_, m // per, q], qkT[g][rows_, 2 + m // per, kk]

                    def score(u):
                        g, t = UNITS[u]
                        for n, maps in enumerate(score_maps(u)):
                            bank = fill("v", "scores", u, n)
                            if n == 0:
                                for tt in range(T):
                                    if g == "mla":
                                        v_done("qkT", g, tt, 1)
                                    else:
                                        v_done("qkT", g, tt)
                            for i, m in enumerate(maps):
                                q, k = head_views(g, t, m)
                                last = nc.tensor.matmul(bank[:, i * keys(t):(i + 1) * keys(t)], q, k, start=True, stop=True)
                            last.then_inc(v_filled, 1)

                    def turn_and_weigh(u):
                        g, t = UNITS[u]
                        s = unit_view(u)
                        if g == "diff":
                            pe.wait_ge(combined, u + 1)
                        else:
                            pe.wait_ge(exped, sum(MAPS[UNITS[n][0]] for n in range(u + 1)))
                        blocks = [s[:, (2 * h if g == "diff" else h), k * P:(k + 1) * P] for h in range(HEADS) for k in range(t + 1)]
                        for n in range(turn_jobs(u)):
                            bank = fill("s", "turn", u, n)
                            transposes(bank, blocks[4 * n:4 * n + 4]).then_inc(s_filled, 1)
                        bank = fill("v", "pv", u)
                        s_done("turn", u, turn_jobs(u) - 1)
                        for h in range(HEADS):
                            for k in range(t + 1):
                                v = {"diff": z[:, k, Z_AV + 64 * h:Z_AV + 64 * h + 64],
                                     "dil": z[:, k, Z_DV + 64 * h:Z_DV + 64 * h + 64],
                                     "mla": mv[:, k, h, :]}[g]
                                last = nc.tensor.matmul(bank[:, 64 * h:64 * h + 64], probsT[:, h, k, :], v,
                                                        start=(k == 0), stop=(k == t))
                        last.then_inc(v_filled, 1)

                    turn_heads("diff", Z_AQ)
                    s_done("z", 4, T - 1)
                    score(0)
                    score(1)
                    for t in range(T):
                        pe.wait_ge(latents_ready, t + 1)
                        bank = fill("v", "cT", t)
                        transposes(bank, [cn[:, t, j * P:(j + 1) * P] for j in range(3)]).then_inc(v_filled, 1)
                    pe.wait_ge(small_loaded, 7 * 16)
                    for t in range(T):
                        bank = fill("s", "mq", t)
                        v_done("cT", t)
                        for j in range(2):
                            last = nc.tensor.matmul(bank[:, 0:HEADS * MQ], cT[:, j, t * P:(t + 1) * P], uq_sb[:, j, :],
                                                    start=(j == 0), stop=(j == 1))
                        last.then_inc(s_filled, 1)
                    for t in range(T):
                        bank = fill("s", "mkv", t)
                        nc.tensor.matmul(bank[:, :], cT[:, 2, t * P:(t + 1) * P], ukv_sb[:, :],
                                         start=True, stop=True).then_inc(s_filled, 1)
                    turn_heads("dil", Z_DQ)
                    turn_and_weigh(0)
                    score(2)
                    turn_and_weigh(1)
                    score(3)
                    pe.wait_ge(rotated["mla"], 1)
                    for t in range(T):
                        for j, src in enumerate((mq, mk)):
                            bank = fill("v", "qkT", "mla", t, j)
                            transposes(bank, [src[:, t, h, :] for h in range(HEADS)], rows_out=MQ).then_inc(v_filled, 1)
                    turn_and_weigh(2)
                    score(4)
                    turn_and_weigh(3)
                    score(5)
                    pe.wait_ge(sgu_masked, 1)
                    for t in range(T):
                        bank = fill("v", "sgu", t)
                        pe.wait_ge(gate_normed, t + 1)
                        for g in range(4):
                            last = nc.tensor.matmul(bank[:, 64 * g:64 * g + 64], sgu_sb[:, g, :],
                                                    z[:, t, Z_V + 64 * g:Z_V + 64 * g + 64], start=True, stop=True)
                        last.then_inc(v_filled, 1)
                    turn_and_weigh(4)
                    turn_and_weigh(5)
                    for t in range(T):
                        pe.wait_ge(mix_ready, t + 1)
                        for j in range(2):
                            bank = fill("v", "mixT", t, j)
                            transposes(bank, [mix[:, t, k * P:(k + 1) * P] for k in range(4 * j, 4 * j + 4)]).then_inc(v_filled, 1)
                    for c in range(2):
                        n = 5 + c
                        pe.wait_ge(chunk_loaded[n % W_SLOTS], 16 * (n // W_SLOTS + 1))
                        for t in range(T):
                            bank = fill("v", "proj", c, t)
                            v_done("mixT", t, 1)
                            for k in range(KC):
                                last = nc.tensor.matmul(bank[:, :], hT[:, k, t * P:(t + 1) * P], ring[:, n % W_SLOTS, k, :],
                                                        start=(k == 0), stop=(k == KC - 1))
                            last.then_inc(v_filled, 1)
                    for t in range(T):
                        pe.wait_ge(h2_ready, t + 1)
                        for j in range(2):
                            bank = fill("s", "h2T", t, j)
                            transposes(bank, [wide[:, t, k * P:(k + 1) * P] for k in range(4 * j, 4 * j + 4)]).then_inc(s_filled, 1)
                    for j in range(4):
                        n = 7 + j // 2
                        bank = fill("s", "peerq", j)
                        if j == 0:
                            s_done("h2T", T - 1, 1)
                        pe.wait_ge(chunk_loaded[n % W_SLOTS], 16 * (n // W_SLOTS + 1))
                        for i in range(2):
                            at = (2 * j + i) % 4 * P
                            for k in range(KC):
                                last = nc.tensor.matmul(bank[:, i * S:(i + 1) * S], ring[:, n % W_SLOTS, k, at:at + P], hT[:, k, :],
                                                        start=(k == 0), stop=(k == KC - 1))
                        last.then_inc(s_filled, 1)
                    for t in range(T):
                        for j in range(4):
                            bank = fill("s", "keys", t, j)
                            s_done("peerq", j // 2 * 2 + 1)
                            for i in range(4):
                                h, half = j // 2 * 4 + i, j % 2
                                part = slice(64 * half, 64 * half + 64)
                                last = nc.tensor.matmul(bank[:, i * P:(i + 1) * P], peer_qT[part, h, t * P:(t + 1) * P],
                                                        keys_sb[part, :], start=True, stop=True)
                            last.then_inc(s_filled, 1)

                @block.vector
                def _(dve):
                    own = Counted(dve)
                    V = nc.vector
                    taken_jobs = []

                    def take(*job):
                        n = len(taken_jobs)
                        assert V_JOBS[n] == job, (V_JOBS[n], job)
                        taken_jobs.append(job)
                        dve.wait_ge(v_filled, n + 1)
                        return v_bank[n % 4]

                    def mean(name, at, n, src, width):
                        first = POWERS[name][0] + at
                        return V.tensor_scalar(ms[:, first:first + n], src, 1.0 / width, EPS, ALU.mult, ALU.add)

                    def stat(name, at, n=1):
                        first = POWERS[name][0] + at
                        return rstd[:, first:first + n]

                    def wait_rstd(name):
                        dve.wait_ge(rstd_ready, POWER_AT[name] + 1)

                    dve.wait_ge(squared, T)
                    own.link(mean("mix_in", 0, 2, sumsq[:, 0:2], D), ms_ready)
                    dve.wait_ge(small_loaded, 7 * 16)
                    lv = row[:, R_LAM:NROW].rearrange("p (a b e) -> p a b e", a=2, b=2)
                    own.link(V.tensor_tensor(lam_prod[:, :, :], lv[:, :, 0, :], lv[:, :, 1, :], ALU.mult), vector_step)
                    own.link(V.tensor_reduce(lam_sum[:, :], lam_prod[:, :, :], AX, ALU.add), lam_summed)
                    wait_rstd("mix_in")
                    for t in range(T):
                        own.link(V.tensor_scalar(wide[:, t, :], x[:, t, :], stat("mix_in", t), None, ALU.mult), h_ready)
                    dve.wait_ge(lam_exped, 1)
                    own.link(V.tensor_tensor(lam[:, :], lam_exp[:, 0:1], lam_exp[:, 1:2], ALU.subtract), vector_step)
                    own.link(V.tensor_tensor(lam[:, :], lam[:, :], lay[:, 0:1], ALU.add), vector_step)
                    own.link(V.tensor_scalar(col[:, C_OUT:C_OUT + 2], col[:, C_OUT:C_OUT + 2], lay[:, 1:2], None, ALU.mult), vector_step)

                    def empty_with_gain(bank, dst, gains, n):
                        own.link(V.tensor_tensor(dst, bank[:, 0:n * P].rearrange("p (k q) -> p k q", k=n), bc(gains, 2, P), ALU.mult), v_emptied)

                    for t in range(T):
                        for j in range(2):
                            empty_with_gain(take("hT", t, j), hT[:, 4 * j:4 * j + 4, t * P:(t + 1) * P],
                                            col[:, C_MIX + 4 * j:C_MIX + 4 * j + 4], 4)
                    dve.wait_ge(squared, T + 4)
                    sums = sumsq[:, 2:6].rearrange("p (t j) -> p t j", j=2)
                    for j, width in enumerate((256, 128)):
                        first = POWERS["latent"][0]
                        dst = ms[:, first:first + 4].rearrange("p (t j) -> p t j", j=2)[:, :, j]
                        own.link(V.tensor_scalar(dst, sums[:, :, j], 1.0 / width, EPS, ALU.mult, ALU.add),
                                 ms_ready if j else vector_step)
                    wait_rstd("latent")
                    for t in range(T):
                        own.link(V.tensor_scalar(cn[:, t, 0:256], z[:, t, Z_CQ:Z_CQ + 256], stat("latent", 2 * t), None, ALU.mult), vector_step)
                        own.link(V.tensor_scalar(cn[:, t, 256:384], z[:, t, Z_CQ + 256:Z_CQ + 384], stat("latent", 2 * t + 1), None, ALU.mult), latents_ready)

                    def copy_heads(g, t):
                        own.link(V.tensor_copy(qkT[g][:, :, t * P:(t + 1) * P],
                                               take("qkT", g, t)[:, :].rearrange("p (b q) -> p b q", b=4)), v_emptied)

                    def mask(u):
                        g, t = UNITS[u]
                        s, kk = unit_view(u), keys(t)
                        if u >= 2:
                            dve.wait_ge(s_filled, S_AT["turn", u - 2, turn_jobs(u - 2) - 1] + 1)
                        m = mask_sb[:, 1 if g == "dil" else 0, t, 0:kk]
                        by_row = s.rearrange("p (a r) k -> p a r k", r=ROW_TILES[g])
                        for n, maps in enumerate(score_maps(u)):
                            bank, per, a = take("scores", u, n), len(maps), maps[0] // ROW_TILES[g]
                            own.link(V.scalar_tensor_tensor(by_row[:, a:a + per, maps[0] % ROW_TILES[g], :],
                                                            bank[:, 0:per * kk].rearrange("p (m k) -> p m k", m=per), SCALE[g],
                                                            bc(m, 1, per), ALU.mult, ALU.add), v_emptied)
                        own.link(V.tensor_reduce(neg_max[:, u % 2, 0:MAPS[g]], s, AX, ALU.max, negate=True), masked)

                    def normalise(u):
                        g, t = UNITS[u]
                        b = u % 2
                        dve.wait_ge(exped, sum(MAPS[UNITS[n][0]] for n in range(u + 1)))
                        own.link(V.reciprocal(rden[:, b, 0:MAPS[g]], den[:, b, 0:MAPS[g]]), vector_step)
                        if g != "diff":
                            return
                        second = rden[:, b, :].rearrange("p (h m) -> p h m", m=2)[:, :, 1]
                        own.link(V.tensor_scalar(second, second, lam[:, 0:1], None, ALU.mult), vector_step)
                        s = unit_view(u)
                        for h in range(HEADS):
                            own.link(V.tensor_scalar(s[:, 2 * h + 1, :], s[:, 2 * h + 1, :], rden[:, b, 2 * h + 1:2 * h + 2], None, ALU.mult), vector_step)
                        for h in range(HEADS):
                            ins = V.scalar_tensor_tensor(s[:, 2 * h, :], s[:, 2 * h, :], rden[:, b, 2 * h:2 * h + 1],
                                                         s[:, 2 * h + 1, :], ALU.mult, ALU.subtract)
                            own.link(ins, combined if h == HEADS - 1 else vector_step)

                    def weighed(u):
                        g, t = UNITS[u]
                        bank = take("pv", u)
                        dst = mix[:, t, MIX_AT[g]:MIX_AT[g] + GROUP]
                        if g == "diff":
                            own.link(V.tensor_copy(dst, bank[:, 0:GROUP]), v_emptied)
                        else:
                            own.link(V.tensor_tensor(dst.rearrange("p (h e) -> p h e", h=HEADS),
                                                     bank[:, 0:GROUP].rearrange("p (h e) -> p h e", h=HEADS),
                                                     bc(rden[:, u % 2, 0:HEADS], 2, 64), ALU.mult), v_emptied)

                    for t in range(T):
                        copy_heads("diff", t)
                    mask(0)
                    mask(1)
                    for t in range(T):
                        empty_with_gain(take("cT", t), cT[:, :, t * P:(t + 1) * P], col[:, C_QKV:C_QKV + 3], 3)
                    dve.wait_ge(squared, T + 4 + T)
                    own.link(mean("gate", 0, 2, sumsq[:, 6:8], GROUP), ms_ready)
                    wait_rstd("gate")
                    for t in range(T):
                        v = z[:, t, Z_V:Z_V + GROUP]
                        own.link(V.scalar_tensor_tensor(v, v, stat("gate", t), row[:, R_SGU:R_SGU + GROUP], ALU.mult, ALU.mult), gate_normed)
                    for t in range(T):
                        copy_heads("dil", t)
                    normalise(0)
                    weighed(0)
                    mask(2)
                    normalise(1)
                    weighed(1)
                    mask(3)
                    for t in range(T):
                        for j in range(2):
                            own.link(V.tensor_copy(qkT["mla"][0:MQ, 4 * j:4 * j + 4, t * P:(t + 1) * P],
                                                   take("qkT", "mla", t, j)[0:MQ, :].rearrange("p (b q) -> p b q", b=4)), v_emptied)
                    normalise(2)
                    weighed(2)
                    mask(4)
                    normalise(3)
                    weighed(3)
                    mask(5)
                    for t in range(T):
                        bank = take("sgu", t)
                        for g in range(4):
                            at = 64 * g
                            ins = V.scalar_tensor_tensor(mix[:, t, 2 * GROUP + at:2 * GROUP + at + 64], bank[:, at:at + 64],
                                                         col[:, C_SGUB + g:C_SGUB + g + 1], z[:, t, Z_U + at:Z_U + at + 64],
                                                         ALU.add, ALU.mult)
                            own.link(ins, v_emptied if g == 3 else vector_step)
                    normalise(4)
                    weighed(4)
                    own.link(V.tensor_copy(sumsq[:, 40:41], sumsq[:, 0:1]), mix_done)
                    normalise(5)
                    weighed(5)
                    own.link(V.tensor_copy(sumsq[:, 41:42], sumsq[:, 0:1]), mix_done)
                    for t in range(T):
                        dve.wait_ge(mix_squared, t + 1)
                        sq = scores[:, t, 0:D]
                        first = POWERS["mixed"][0] + 7 * t
                        own.link(V.tensor_reduce(sumsq[:, 12 + 7 * t:16 + 7 * t], sq[:, 0:GROUP].rearrange("p (h e) -> p h e", h=HEADS), AX, ALU.add), vector_step)
                        own.link(V.tensor_reduce(sumsq[:, 16 + 7 * t:19 + 7 * t], sq[:, GROUP:D].rearrange("p (h e) -> p h e", h=3), AX, ALU.add), vector_step)
                        own.link(V.tensor_scalar(ms[:, first:first + 4], sumsq[:, 12 + 7 * t:16 + 7 * t], 1.0 / 64, EPS, ALU.mult, ALU.add), vector_step)
                        own.link(V.tensor_scalar(ms[:, first + 4:first + 7], sumsq[:, 16 + 7 * t:19 + 7 * t], 1.0 / GROUP, EPS, ALU.mult, ALU.add),
                                 ms_ready if t == T - 1 else vector_step)
                    wait_rstd("mixed")
                    for t in range(T):
                        a = mix[:, t, 0:GROUP].rearrange("p (h e) -> p h e", h=HEADS)
                        own.link(V.tensor_tensor(a, a, bc(stat("mixed", 7 * t, 4), 2, 64), ALU.mult), vector_step)
                        b = mix[:, t, GROUP:D].rearrange("p (h e) -> p h e", h=3)
                        own.link(V.tensor_tensor(b, b, bc(stat("mixed", 7 * t + 4, 3), 2, GROUP), ALU.mult), mix_ready)
                    for t in range(T):
                        for j in range(2):
                            empty_with_gain(take("mixT", t, j), hT[:, 4 * j:4 * j + 4, t * P:(t + 1) * P],
                                            col[:, C_OUT + 4 * j:C_OUT + 4 * j + 4], 4)
                    for c in range(2):
                        for t in range(T):
                            bank = take("proj", c, t)
                            part = x[:, t, c * CH:(c + 1) * CH]
                            own.link(V.tensor_tensor(part, part, bank[:, :], ALU.add), v_emptied)
                            if c == 1:
                                own.link(V.tensor_copy(sumsq[:, 42:43], sumsq[:, 0:1]), x_ready)
                    dve.wait_ge(squared, 2 * T + 4 + T)
                    own.link(mean("ffn", 0, 2, sumsq[:, 8:10], D), ms_ready)
                    wait_rstd("ffn")
                    for t in range(T):
                        own.link(V.scalar_tensor_tensor(wide[:, t, :], x[:, t, :], stat("ffn", t), row[:, R_FFN:R_FFN + D], ALU.mult, ALU.mult), h2_ready)

                    def top16(values, numbers, src):
                        for r in range(2):
                            own.link(V.max(values[:, 8 * r:8 * r + 8], src), vector_step)
                            own.link(V.max_index(numbers[:, 8 * r:8 * r + 8], values[:, 8 * r:8 * r + 8], src), vector_step)
                            if r == 0:
                                own.link(V.match_replace(src, values[:, 0:8], src, LOWEST), vector_step)

                    def choose(t):
                        for j in range(2):
                            dve.wait_ge(s_emptied, S_AT["keys", t, 2 * j + 1] + 1)
                            for i in range(8 * j, 8 * j + 8):
                                top16(top_v[:, i, :], top_i[:, i, :], key_scores[:, t, i, :])
                        own.link(V.tensor_copy(top_f[:, :, :], top_i[:, :, :]), vector_step)
                        tv = top_v[:, :, :].rearrange("p (h c) k -> p h c k", c=2)
                        tf = top_f[:, :, :].rearrange("p (h c) k -> p h c k", c=2)
                        own.link(V.tensor_tensor(pairs, bc(tv[:, :, 0, :], 3, TOPK), bc(tv[:, :, 1, :], 2, TOPK), ALU.add), vector_step)
                        for h in range(PH):
                            top16(best[:, t, h, :], pos[:, h, :], pairs[:, h, :, :].rearrange("p i j -> p (i j)"))
                        own.link(V.tensor_tensor(gate[:, t, :, :], best[:, t, :, :], best[:, t, :, 0:1].to_broadcast([P, PH, TOPK]), ALU.subtract), shifted)
                        own.link(V.tensor_scalar(pos_hi[:, :, :], pos[:, :, :], 4, None, ALU.logical_shift_right), vector_step)
                        own.link(V.tensor_copy(pos_hi_f[:, :, :], pos_hi[:, :, :]), vector_step)
                        own.link(V.tensor_scalar(pos[:, :, :], pos[:, :, :], TOPK - 1, None, ALU.bitwise_and), vector_step)
                        own.link(V.tensor_copy(pos_f[:, :, :], pos[:, :, :]), vector_step)
                        hk = onehot.rearrange("p h k i -> p (h k) i")
                        for c, which in enumerate((pos_hi_f, pos_f)):
                            w = which[:, :, :].rearrange("p h k -> p (h k)")
                            own.link(V.tensor_tensor(hk, bc(iota16[:, :], 1, PICKS), bc(w, 2, TOPK), ALU.is_equal), vector_step)
                            own.link(V.tensor_tensor(onehot, onehot, bc(tf[:, :, c, :], 2, TOPK), ALU.mult), vector_step)
                            own.link(V.tensor_reduce(key_of[:, c, :, :].rearrange("p h k -> p (h k)"), hk, AX, ALU.add), vector_step)
                        k0 = key_of[:, 0, :, :].rearrange("p h k -> p (h k)")
                        k1 = key_of[:, 1, :, :].rearrange("p h k -> p (h k)")
                        own.link(V.scalar_tensor_tensor(expert_f[:, :], k0, float(NKEY), k1, ALU.mult, ALU.add), vector_step)
                        own.link(V.tensor_scalar(expert[:, t, :], expert_f[:, :], lay[:, 2:3], None, ALU.add), experts_ready)

                    for t in range(T):
                        choose(t)
                    for t in range(T):
                        dve.wait_ge(gates_exped, t + 1)
                        own.link(V.tensor_reduce(gate_sum[:, :], gate[:, t, :, :], AX, ALU.add), vector_step)
                        own.link(V.reciprocal(gate_sum[:, :], gate_sum[:, :]), vector_step)
                        own.link(V.tensor_tensor(gate[:, t, :, :], gate[:, t, :, :], bc(gate_sum[:, :], 2, TOPK), ALU.mult), vector_step)

                    for t in range(T):
                        with dve.Fori(0, GROUPS) as g:
                            for b in range(SLOTS):
                                dve.wait_ge(row_loaded[b], (layer * (2 * T * GROUPS) + g + 2 * t * GROUPS) * 16 + 16)
                                V.scalar_tensor_tensor(gathered[:, b, :], gathered[:, b, :], 1.0, wide[:, t, :], ALU.mult, ALU.mult,
                                                       accum_out=dots[:, t, bass.ds(g * SLOTS + b, 1)]).then_inc(slots_free, 1)
                        dve.wait_ge(slots_free, SLOTS + (2 * t + 1) * PICKS)
                        own.link(V.tensor_copy(sumsq[:, 43:44], sumsq[:, 0:1]), dots_done)
                        dve.wait_ge(dots_gelud, t + 1)
                        own.link(V.tensor_tensor(act_dots[:, t, :], act_dots[:, t, :], gate[:, t, :, :].rearrange("p h k -> p (h k)"), ALU.mult), vector_step)
                        with dve.Fori(0, GROUPS) as g:
                            for b in range(SLOTS):
                                dve.wait_ge(slots_free, g * SLOTS + (SLOTS + (2 * t + 1) * PICKS + b))
                                dve.wait_ge(row_loaded[b], (layer * (2 * T * GROUPS) + g + (2 * t + 1) * GROUPS) * 16 + 16)
                                V.scalar_tensor_tensor(x[:, t, :], gathered[:, b, :], act_dots[:, t, bass.ds(g * SLOTS + b, 1)],
                                                       x[:, t, :], ALU.mult, ALU.add).then_inc(slots_free, 1)
                    dve.wait_ge(slots_free, SLOTS + 2 * T * PICKS)

                @block.gpsimd
                def _(pool):
                    own = Counted(pool)
                    G = nc.gpsimd
                    G.sem_inc(slots_free, SLOTS)

                    def power(name):
                        first, n = POWERS[name]
                        pool.wait_ge(ms_ready, POWER_AT[name] + 1)
                        own.link(G.tensor_tensor(rstd[:, first:first + n], ms[:, first:first + n], half_neg[:, 0:n], ALU.pow), rstd_ready)

                    def rotate(view, n, half, at, done):
                        cos = bc(rope_sb[:, 0, :, at:at + half], 2, n)
                        sin = bc(rope_sb[:, 1, :, at:at + half], 2, n)
                        low, high = view[:, :, :, 0:half], view[:, :, :, half:2 * half]
                        part = [rot[:, i, 0:T * n * half].rearrange("p (t n e) -> p t n e", t=T, n=n) for i in range(4)]
                        own.go(G.tensor_tensor(part[0], low, cos, ALU.mult), gpsimd_step)
                        own.go(G.tensor_tensor(part[1], high, sin, ALU.mult), gpsimd_step)
                        own.go(G.tensor_tensor(part[2], high, cos, ALU.mult), gpsimd_step)
                        own.link(G.tensor_tensor(part[3], low, sin, ALU.mult), gpsimd_step)
                        own.go(G.tensor_tensor(low, part[0], part[1], ALU.subtract), gpsimd_step)
                        own.link(G.tensor_tensor(high, part[2], part[3], ALU.add), done)
                        pool.wait_ge(gpsimd_step, own.value[id(gpsimd_step)])

                    power("mix_in")
                    pool.wait_ge(small_loaded, 7 * 16)
                    own.link(G.tensor_tensor(sgu_sb[:, :, :], sgu_sb[:, :, :], bc(tri_sb[:, :], 1, 4), ALU.mult), sgu_masked)
                    pool.wait_ge(s_emptied, S_AT["z", 0, T - 1] + 1)
                    rotate(z[:, :, 0:512].rearrange("p t (n e) -> p t n e", e=32), 16, 4, 0, rotated["diff"])
                    power("latent")
                    kpe = z[:, :, Z_KPE:Z_KPE + 32].rearrange("p t (n e) -> p t n e", n=1)
                    rotate(kpe, 1, 16, 12, gpsimd_step)
                    pool.wait_ge(s_emptied, S_AT["z", 4, T - 1] + 1)
                    rotate(z[:, :, Z_DQ:Z_DQ + 512].rearrange("p t (n e) -> p t n e", e=64), 8, 8, 4, rotated["dil"])
                    power("gate")
                    pool.wait_ge(s_emptied, S_AT["mkv", T - 1] + 1)
                    pool.wait_ge(scalar_step, T)
                    rotate(mq[:, :, :, 64:MQ], HEADS, 16, 12, gpsimd_step)
                    kpe_all = z[:, :, Z_KPE:Z_KPE + 32]
                    for t in range(T):
                        own.go(G.tensor_copy(mk[:, t, :, 64:MQ], bc(kpe_all[:, t, :], 1, HEADS)), gpsimd_step)
                    pool.wait_ge(gpsimd_step, own.value[id(gpsimd_step)])
                    own.link(G.tensor_copy(rot[:, 0, 0:1], rot[:, 0, 1:2]), rotated["mla"])
                    power("mixed")
                    power("ffn")

                    for t in range(T):
                        for half, table in enumerate((experts_u, experts_v)):
                            phase = 2 * t + half
                            pool.wait_ge(experts_ready, t + 1)
                            with pool.Fori(0, GROUPS) as g:
                                for b in range(SLOTS):
                                    n = g * SLOTS + (phase * PICKS + b)
                                    pool.wait_ge(slots_free, n + 1)
                                    G.sem_inc(gather_turn, 1)
                                    G.tensor_copy(index_slot[:, b:b + 1], expert[:, t, bass.ds(g * SLOTS + b, 1)]).then_inc(index_copied, 1)
                                    pool.wait_ge(index_copied, n + 1)
                                    G.sem_inc(gather_turn, 1)
                                    G.indirect_dma_start(gathered[:, b, :], None, table,
                                                         bass.IndirectOffsetOnAxis(ap=index_slot[:, b:b + 1], axis=0)).then_inc(row_loaded[b], 16)

            for s in taken:
                nc.gpsimd.sem_clear(s)
            nc.all_engine_barrier()

        final_sum, final_row = ctx.enter_context(nc.semaphore("final_sum")), ctx.enter_context(nc.semaphore("final_row"))
        final_ms, final_rstd = ctx.enter_context(nc.semaphore("final_ms")), ctx.enter_context(nc.semaphore("final_rstd"))
        final_out = ctx.enter_context(nc.semaphore("final_out"))
        first = POWERS["final"][0]
        with nc.Block() as block:
            @block.sync
            def _(sp):
                gain = final_gain.rearrange("(o n) -> o n", o=1).to_broadcast([P, D])
                sp.dma_start(row[:, 0:D], gain).then_inc(final_row, 16)
                for t in range(T):
                    sp.wait_ge(final_out, t + 1)
                    sp.dma_start(out[t * P:(t + 1) * P, :], wide[:, t, :]).then_inc(stored, 16)
                sp.wait_ge(stored, 16 * T)

            @block.scalar
            def _(act):
                for t in range(T):
                    nc.scalar.activation(z[:, t, 0:D], x[:, t, :], ACT.Square, accum_out=sumsq[:, t:t + 1]).then_inc(final_sum, 1)

            @block.gpsimd
            def _(pool):
                pool.wait_ge(final_ms, 1)
                nc.gpsimd.tensor_tensor(rstd[:, first:first + T], ms[:, first:first + T], half_neg[:, 0:T], ALU.pow).then_inc(final_rstd, 1)

            @block.vector
            def _(dve):
                dve.wait_ge(final_sum, T)
                nc.vector.tensor_scalar(ms[:, first:first + T], sumsq[:, 0:T], 1.0 / D, EPS, ALU.mult, ALU.add).then_inc(final_ms, 1)
                dve.wait_ge(final_rstd, 1)
                dve.wait_ge(final_row, 16)
                for t in range(T):
                    nc.vector.scalar_tensor_tensor(wide[:, t, :], x[:, t, :], rstd[:, first + t:first + t + 1], row[:, 0:D],
                                                   ALU.mult, ALU.mult).then_inc(final_out, 1)


def shape_constants(seq):
    P, T = 128, seq // 128
    q = np.arange(seq)[:, None]
    k = np.arange(256)[None, :]
    causal = np.where(k <= q, 0.0, -1e30).astype(np.float32)
    count = np.zeros((seq, 256))
    for window, dil in ((128, 1), (512, 4), (2048, 16)):
        d = q - k
        count += (d >= 0) & (d % dil == 0) & (d // dil <= window // dil)
    dilated = np.where(count > 0, np.log(np.maximum(count, 1)), -1e30).astype(np.float32)
    masks = np.stack([causal, dilated]).reshape(2, T, P, 256).transpose(2, 0, 1, 3)
    angles = []
    for n_rot in (8, 16, 32):
        inv = np.float32(500000.0) ** (-np.arange(n_rot // 2, dtype=np.float32) * np.float32(2.0 / n_rot))
        angles.append(np.arange(seq, dtype=np.float32)[:, None] * inv[None, :])
    angles = np.concatenate(angles, 1).astype(np.float32)
    rope = np.stack([np.cos(angles), np.sin(angles)]).reshape(2, T, P, 28).transpose(2, 0, 1, 3)
    return {
        "masks": np.ascontiguousarray(masks), "rope": np.ascontiguousarray(rope),
        "triangle": np.triu(np.ones((P, P), np.float32)), "identity": np.eye(P, dtype=np.float32),
    }


def kernel(x, w_in, w_out, norm_mix, norm_ffn, diff_lambda, diff_head_norm, mla_q_norm, mla_kv_norm,
           mla_w_uq, mla_w_ukv, mla_out_norm, sgu_v_norm, sgu_w, sgu_b, sgu_out_norm, dil_out_norm,
           peer_w_q, peer_sub_keys, peer_u, peer_v, final_norm):
    import concourse.bacc as _bacc
    from concourse.bass_utils import run_bass_kernel_spmd as _run

    A = np.asarray
    L, seq, D = w_in.shape[0], x.shape[1], x.shape[2]
    n_experts = peer_u.shape[1]

    def down(a):
        a = A(a)
        return a.reshape(L, -1, 128).transpose(0, 2, 1)

    lam_init = [0.8 - 0.6 * math.exp(-0.3 * l) for l in range(L)]
    layer_consts = np.array([[v, 1.0 - v, l * n_experts] for l, v in enumerate(lam_init)], np.float32)
    arrays = {
        "x_in": A(x).reshape(seq, D), "w_in": A(w_in), "w_out": A(w_out), "w_q": A(peer_w_q),
        "columns": np.concatenate([down(norm_mix), down(mla_q_norm), down(mla_kv_norm), down(diff_head_norm),
                                   down(mla_out_norm), down(sgu_out_norm), down(dil_out_norm),
                                   A(sgu_b).transpose(0, 2, 1)], 2),
        "rows": np.concatenate([A(sgu_v_norm), A(norm_ffn), A(diff_lambda).reshape(L, -1)], 1),
        "layer_consts": np.repeat(layer_consts[:, None, :], 128, 1),
        "w_uq": A(mla_w_uq), "w_ukv": A(mla_w_ukv),
        "sgu_wt": A(sgu_w).transpose(0, 3, 1, 2), "keys_t": A(peer_sub_keys).transpose(0, 1, 3, 2).reshape(L, 128, -1),
        "experts_u": A(peer_u).reshape(L * n_experts, D), "experts_v": A(peer_v).reshape(L * n_experts, D),
        "final_gain": A(final_norm),
    }
    arrays.update(shape_constants(seq))
    nc = _bacc.Bacc("TRN2", target_bir_lowering=False, num_devices=1)
    feeds, args = {}, []
    for name, a in arrays.items():
        a = np.ascontiguousarray(a)
        feeds[f"in_{name}"] = a
        args.append(nc.dram_tensor(f"in_{name}", a.shape, mybir.dt.from_np(a.dtype), kind="ExternalInput").ap())
    args.append(nc.dram_tensor("out_0", (seq, D), mybir.dt.float32, kind="ExternalOutput").ap())
    bass_hybrid_trunk_peer(nc, *args)
    r = _run(nc, [feeds], core_ids=[0])
    return r.results[0]["out_0"].reshape(1, seq, D)
```

```python
import math
from contextlib import ExitStack

import numpy as np
import concourse.bass as bass
from concourse import mybir


def bass_hybrid_trunk_peer(
    nc: bass.Bass,
    x_in: bass.AP,
    w_in: bass.AP,
    w_out: bass.AP,
    w_q: bass.AP,
    columns: bass.AP,
    rows: bass.AP,
    ffn_gains: bass.AP,
    layer_consts: bass.AP,
    w_uq: bass.AP,
    w_ukv: bass.AP,
    sgu_wt: bass.AP,
    keys_t: bass.AP,
    experts_u: bass.AP,
    experts_v: bass.AP,
    final_gain: bass.AP,
    masks: bass.AP,
    rope: bass.AP,
    triangle: bass.AP,
    identity: bass.AP,
    out: bass.AP,
):
    fp32 = mybir.dt.float32
    u32 = mybir.dt.uint32
    ALU = mybir.AluOpType
    ACT = mybir.ActivationFunctionType
    AX = mybir.AxisListType.X

    P = 128
    L = w_in.shape[0]
    D = x_in.shape[1]
    T = x_in.shape[0] // P
    S = x_in.shape[0]
    KC = D // P
    IN_W = w_in.shape[2]
    CH = 512
    EPS = 1e-6
    GROUP = D // 4
    Z_AQ, Z_AV, Z_CQ, Z_KPE, Z_U, Z_V, Z_DQ, Z_DV = 0, 512, 768, 1152, 1184, 1440, 1696, 2208
    C_MIX, C_QKV, C_OUT, C_SGUB, NCOL = 0, 8, 11, 19, 23
    R_SGU, R_LAM, NROW = 0, GROUP, GROUP + 128
    HEADS = 4
    MQ = 96
    PH, TOPK, NKEY = 8, 16, 128
    PICKS = PH * TOPK
    SLOTS = 8
    ROUNDS = PICKS // SLOTS
    NW = 8
    WC = IN_W // NW
    W_SLOTS = 2
    LOWEST = -3.0e38
    PE_SLOTS = list(range(1, SLOTS, 2))
    DVE_SLOTS = list(range(0, SLOTS, 2))
    HALF = SLOTS // 2
    BANKS = 3

    GROUPS = ("diff", "dil", "mla")
    MAPS = {"diff": 8, "dil": 4, "mla": 4}
    SCALE = {"diff": 32 ** -0.5, "dil": 64 ** -0.5, "mla": MQ ** -0.5}
    MIX_AT = {"diff": 0, "mla": GROUP, "dil": 3 * GROUP}
    ROW_TILES = {"diff": 4, "dil": 2, "mla": 1}

    def keys(t):
        return P * (t + 1)

    def score_maps(g, t):
        r, per = ROW_TILES[g], min(MAPS[g] // ROW_TILES[g], CH // keys(t))
        return [list(range(i + n * per * r, MAPS[g], r))[:per] for n in range(MAPS[g] // r // per) for i in range(r)]

    def v_jobs(t):
        def of(g):
            return [("scores", g, n) for n in range(len(score_maps(g, t)))]
        jobs = [("hT", 0), ("hT", 1)] + of("diff") + [("cT",)] + of("dil") + [("pv", "diff")] + of("mla")
        jobs += [("pv", "dil"), ("sgu",), ("pv", "mla"), ("mixT", 0), ("mixT", 1), ("proj", 0), ("proj", 1)]
        return jobs

    def s_jobs(t):
        def turn(g):
            return [("turn", g, n) for n in range(t + 1)]
        jobs = [("z", c) for c in range(NW)] + [("qkT", "diff"), ("mq",), ("mkv",), ("qkT", "dil")] + turn("diff")
        jobs += [("mlaT", 0), ("mlaT", 1)] + turn("dil") + turn("mla")
        jobs += [("h2T", 0), ("h2T", 1)] + [("peerq", j) for j in range(2)] + [("keys", j) for j in range(4)]
        return jobs

    POWERS = {"mix_in": (0, 1), "latent": (1, 2), "gate": (3, 1), "mixed": (4, 7), "ffn": (11, 1), "final": (12, 2)}
    POWER_AT = {name: n for n, name in enumerate(POWERS)}

    ctx = ExitStack()
    with ctx:
        def sb(name, shape, dt=fp32):
            return ctx.enter_context(nc.sbuf_tensor(name, shape, dt))

        taken = []

        def sem(name):
            s = ctx.enter_context(nc.semaphore(name))
            taken.append(s)
            return s

        x = sb("x", [P, T, D])
        wide = sb("wide", [P, T, D])
        hT = sb("hT", [P, KC, P])
        z = sb("z", [P, IN_W])
        ring = sb("ring", [P, W_SLOTS, KC, WC])
        w_kept = sb("w_kept", [P, 4, KC, CH])
        gathered = sb("gathered", [P, SLOTS, D])
        scores = sb("scores", [P, 2, 8 * 256])
        qT = {"diff": sb("qT_diff", [P, 2, P]), "dil": sb("qT_dil", [P, 2, P]), "mla": sb("qT_mla", [P, 4, P])}
        kT = {"diff": sb("kT_diff", [P, 2, S]), "dil": sb("kT_dil", [P, 2, S]), "mla": sb("kT_mla", [P, 4, S])}
        values = {g: sb(f"values_{g}", [P, T, GROUP]) for g in GROUPS}
        mq = sb("mq", [P, HEADS, MQ])
        mk = sb("mk", [P, HEADS, MQ])
        cn = sb("cn", [P, 3 * P])
        cT = sb("cT", [P, 3, P])
        uq_sb = sb("uq_sb", [P, 2, HEADS * MQ])
        ukv_sb = sb("ukv_sb", [P, 512])
        sgu_sb = sb("sgu_sb", [P, 4, P])
        keys_sb = sb("keys_sb", [P, NKEY])
        col = sb("col", [P, NCOL])
        row = sb("row", [P, NROW])
        lay = sb("lay", [P, 3])
        mask_sb = sb("mask_sb", [P, 2, 3 * P])
        rope_sb = sb("rope_sb", [P, 2, T, 28])
        tri_sb = sb("tri_sb", [P, P])
        id_sb = sb("id_sb", [P, P])
        iota16 = sb("iota16", [P, TOPK])
        iota16_i = sb("iota16_i", [P, TOPK], mybir.dt.int32)
        half_neg = sb("half_neg", [P, 8])
        ms = sb("ms", [P, 14])
        rstd = sb("rstd", [P, 14])
        sumsq = sb("sumsq", [P, 16])
        signal = sb("signal", [P, 4])
        rot = sb("rot", [P, 4, 64])
        neg_max = {g: sb(f"neg_max_{g}", [P, MAPS[g]]) for g in GROUPS}
        den = {g: sb(f"den_{g}", [P, MAPS[g]]) for g in GROUPS}
        rden = {g: sb(f"rden_{g}", [P, MAPS[g]]) for g in GROUPS}
        lam_prod = sb("lam_prod", [P, 2, 32])
        lam_sum = sb("lam_sum", [P, 2])
        lam_exp = sb("lam_exp", [P, 2])
        lam = sb("lam", [P, 1])
        top_i = sb("top_i", [P, 2 * PH, TOPK], u32)
        expert = sb("expert", [P, T, PICKS], u32)
        index_slot = sb("index_slot", [P, SLOTS], u32)
        gate = sb("gate", [P, T, PH, TOPK])
        gate_sum = sb("gate_sum", [P, PH])
        dots = sb("dots", [P, PICKS])
        weights = sb("weights", [P, PICKS])
        diag = sb("diag", [P, HALF, P])
        zeros = sb("zeros", [P, P])

        squares = scores[:, 1, 0:D]
        score_of = {"diff": scores[:, 0, :], "dil": scores[:, 1, 0:D], "mla": scores[:, 1, D:2 * D]}
        probsT = z[:, 0:HEADS * T * P]
        ffn_gain = z[:, Z_V:Z_V + D]
        peer_qT = scores[:, 1, 0:D].rearrange("p (h q) -> p h q", h=PH)
        key_scores = z[:, 0:2 * PH * NKEY].rearrange("p (h n) -> p h n", n=NKEY)
        pairs = scores[:, 0, :].rearrange("p (h i j) -> p h i j", i=TOPK, j=TOPK)
        onehot = scores[:, 1, :].rearrange("p (h k i) -> p h k i", k=TOPK, i=TOPK)
        top_f = cn[:, 0:2 * PH * TOPK].rearrange("p (h k) -> p h k", k=TOPK)
        flat_cT = cT[:, :, :].rearrange("p k q -> p (k q)")
        key_of = flat_cT[:, 0:2 * PICKS].rearrange("p (c h k) -> p c h k", c=2, k=TOPK)
        pos_f = flat_cT[:, 2 * PICKS:3 * PICKS].rearrange("p (h k) -> p h k", k=TOPK)
        top_v = rot[:, :, :].rearrange("p i (h k) -> p (i h) k", k=TOPK)
        flat_mk = mk[:, :, :].rearrange("p h e -> p (h e)")
        best = flat_mk[:, 0:PICKS].rearrange("p (h k) -> p h k", k=TOPK)
        pos = flat_mk[:, PICKS:2 * PICKS].bitcast(u32).rearrange("p (h k) -> p h k", k=TOPK)
        flat_mq = mq[:, :, :].rearrange("p h e -> p (h e)")
        pos_hi_f = flat_mq[:, 0:PICKS].rearrange("p (h k) -> p h k", k=TOPK)
        expert_f = flat_mq[:, PICKS:2 * PICKS]
        pos_hi = flat_mq[:, 2 * PICKS:3 * PICKS].bitcast(u32).rearrange("p (h k) -> p h k", k=TOPK)

        v_bank = [ctx.enter_context(nc.psum_tensor(f"v_bank{i}", [P, CH], fp32)) for i in range(BANKS)]
        s_bank = [ctx.enter_context(nc.psum_tensor(f"s_bank{i}", [P, CH], fp32)) for i in range(BANKS)]
        pe_sum = [ctx.enter_context(nc.psum_tensor(f"pe_sum{i}", [P, CH], fp32)) for i in range(2)]

        const_loaded = ctx.enter_context(nc.semaphore("const_loaded"))
        const_made = ctx.enter_context(nc.semaphore("const_made"))
        stored = ctx.enter_context(nc.semaphore("stored"))
        row_loaded = [ctx.enter_context(nc.semaphore(f"row_loaded{i}")) for i in range(SLOTS)]
        small_loaded = sem("small_loaded")
        ffn_loaded = sem("ffn_loaded")
        chunk_loaded = [sem(f"chunk_loaded{i}") for i in range(W_SLOTS)]
        kept_loaded = [sem(f"kept_loaded{i}") for i in range(4)]
        v_filled, v_emptied = sem("v_filled"), sem("v_emptied")
        s_filled, s_emptied = sem("s_filled"), sem("s_emptied")
        squared = sem("squared")
        ms_ready = sem("ms_ready")
        rstd_ready = sem("rstd_ready")
        vector_step = sem("vector_step")
        gpsimd_step = sem("gpsimd_step")
        values_ready = sem("values_ready")
        queries_turned = sem("queries_turned")
        mk_ready = sem("mk_ready")
        h_ready = sem("h_ready")
        latents_ready = sem("latents_ready")
        lam_summed = sem("lam_summed")
        lam_exped = sem("lam_exped")
        gated = sem("gated")
        gate_normed = sem("gate_normed")
        rotated = {g: sem(f"rotated_{g}") for g in GROUPS}
        sgu_masked = sem("sgu_masked")
        masked = sem("masked")
        exped = {g: sem(f"exped_{g}") for g in GROUPS}
        combined = sem("combined")
        mix_done = sem("mix_done")
        mix_ready = sem("mix_ready")
        x_ready = sem("x_ready")
        h2_ready = sem("h2_ready")
        experts_ready = sem("experts_ready")
        shifted = sem("shifted")
        gates_exped = sem("gates_exped")
        index_copied = sem("index_copied")
        gather_turn = sem("gather_turn")
        slots_free = sem("slots_free")
        pe_slots_free = sem("pe_slots_free")
        pe_summed = sem("pe_summed")
        diag_turn = sem("diag_turn")
        diag_made = sem("diag_made")
        weights_ready = sem("weights_ready")
        dots_done = sem("dots_done")
        dots_gelud = sem("dots_gelud")

        def bc(ap, axis, n):
            a = ap.unsqueeze(axis)
            shape = list(a.shape)
            shape[axis] = n
            return a.to_broadcast(shape)

        class Counted:

            def __init__(self, eng):
                self.eng, self.value = eng, {}

            def go(self, ins, s, n=1):
                ins.then_inc(s, n)
                self.value[id(s)] = self.value.get(id(s), 0) + n

            def link(self, ins, s):
                self.go(ins, s)
                self.eng.wait_ge(s, self.value[id(s)])

        def rounds(eng, first, n, body):
            if n == 1:
                body(first)
            elif n > 1:
                with eng.Fori(first, first + n) as g:
                    body(g)

        def step(pre, gat):
            layer, t = pre if pre else (None, None)
            g_layer, gt = gat if gat else (None, None)
            V_JOBS, S_JOBS = (v_jobs(t), s_jobs(t)) if pre else ([], [])
            V_AT = {job: n for n, job in enumerate(V_JOBS)}
            S_AT = {job: n for n, job in enumerate(S_JOBS)}
            if pre:
                one = slice(layer, layer + 1) if isinstance(layer, int) else bass.ds(layer, 1)
                q_at, kk = slice(t * P, (t + 1) * P), keys(t)
                mix = wide[:, t, :]

            def z_chunk(end):
                return (end - 1) // WC

            def unit_view(g):
                return score_of[g][:, 0:MAPS[g] * kk].rearrange("p (m k) -> p m k", m=MAPS[g])

            def sync_program(sp):
                if not pre:
                    return

                for c in range(NW):
                    if c >= W_SLOTS:
                        sp.wait_ge(s_filled, S_AT["z", c - W_SLOTS] + 1)
                    src = w_in[one].rearrange("o (k p) n -> p (o k) n", p=P)[:, :, c * WC:(c + 1) * WC]
                    sp.dma_start(ring[:, c % W_SLOTS, :, :], src).then_inc(chunk_loaded[c % W_SLOTS], 16)
                if t == 0:
                    for c in range(4):
                        w = (w_out if c < 2 else w_q)[one].rearrange("o (k p) n -> p (o k) n", p=P)
                        sp.dma_start(w_kept[:, c, :, :], w[:, :, c % 2 * CH:(c % 2 + 1) * CH]).then_inc(kept_loaded[c], 16)
                sp.wait_ge(mix_done, 1)
                sp.dma_start(ffn_gain, ffn_gains[one].to_broadcast([P, D])).then_inc(ffn_loaded, 16)

            def scalar_program(act):
                own = Counted(act)
                taken_jobs = []
                A = nc.scalar

                def take(*job):
                    n = len(taken_jobs)
                    assert S_JOBS[n] == job, (S_JOBS[n], job)
                    taken_jobs.append(job)
                    act.wait_ge(s_filled, n + 1)
                    return s_bank[n % BANKS]

                def gelu_dots():
                    if gat:
                        act.wait_ge(dots_done, 1)
                        own.go(A.activation(weights[:, :], dots[:, :], ACT.Gelu_apprx_tanh), dots_gelud)

                made = [0]

                def diag_round(g):
                    for j, b in enumerate(PE_SLOTS):
                        act.wait_ge(pe_slots_free, g * HALF + (j + 1))
                        A.sem_inc(diag_turn, 1)
                        A.activation(diag[:, j, :], id_sb[:, :], ACT.Copy,
                                     scale=weights[:, bass.ds(g * SLOTS + b, 1)]).then_inc(diag_made, 1)

                def make_diags(n):
                    if gat:
                        if not made[0]:
                            act.wait_ge(weights_ready, 1)
                        rounds(act, made[0], n, diag_round)
                        made[0] += n

                if not pre:
                    gelu_dots()
                    make_diags(ROUNDS)
                    return
                if t == 0:
                    act.dma_start(col[:, :], columns[one].rearrange("o p n -> p (o n)")).then_inc(small_loaded, 16)
                    act.dma_start(row[:, :], rows[one].to_broadcast([P, NROW])).then_inc(small_loaded, 16)
                    act.dma_start(lay[:, :], layer_consts[one].rearrange("o p n -> p (o n)")).then_inc(small_loaded, 16)
                    act.dma_start(uq_sb[:, :, :], w_uq[one].rearrange("o (k p) n -> p (o k) n", p=P)).then_inc(small_loaded, 16)
                    act.dma_start(ukv_sb[:, :], w_ukv[one].rearrange("o p n -> p (o n)")).then_inc(small_loaded, 16)
                    act.dma_start(sgu_sb[:, :, :], sgu_wt[one].rearrange("o s g t -> s (o g) t")).then_inc(small_loaded, 16)
                    act.dma_start(keys_sb[:, :], keys_t[one].rearrange("o p n -> p (o n)")).then_inc(small_loaded, 16)

                def square(src, junk, at):
                    own.link(A.activation(junk, src, ACT.Square, accum_out=sumsq[:, at:at + 1]), squared)

                square(x[:, t, :], squares, 0)
                if t == 0:
                    act.wait_ge(lam_summed, 1)
                    own.go(A.activation(lam_exp[:, :], lam_sum[:, :], ACT.Exp), lam_exped)

                def exps(g):
                    act.wait_ge(masked, GROUPS.index(g) + 1)
                    s = unit_view(g)
                    for m in range(MAPS[g]):
                        own.go(A.activation(s[:, m, :], s[:, m, :], ACT.Exp, bias=neg_max[g][:, m:m + 1],
                                            accum_out=den[g][:, m:m + 1]), exped[g])

                def turned(g):
                    flat = probsT[:, 0:HEADS * kk].rearrange("p (h k q) -> p h k q", h=HEADS, k=t + 1)
                    hn = 4 // (t + 1)
                    for n in range(t + 1):
                        bank = take("turn", g, n)
                        own.go(A.activation(flat[:, n * hn:(n + 1) * hn, :, :],
                                            bank[:, :].rearrange("p (h k q) -> p h k q", h=hn, k=t + 1), ACT.Copy), s_emptied)

                def queries_keys(g):
                    bank = take("qkT", g)[:, :].rearrange("p (b q) -> p b q", b=4)
                    own.go(A.activation(qT[g][:, :, :], bank[:, 0:2, :], ACT.Copy), queries_turned)
                    own.go(A.activation(kT[g][:, :, q_at], bank[:, 2:4, :], ACT.Copy), s_emptied)

                def empty_z_until(end):
                    for c in range(emptied_z[0], z_chunk(end) + 1):
                        bank = take("z", c)
                        own.go(A.activation(z[:, c * WC:(c + 1) * WC], bank[:, 0:WC], ACT.Copy), s_emptied)
                    emptied_z[0] = z_chunk(end) + 1
                    act.wait_ge(s_emptied, S_AT["z", z_chunk(end)] + 1)

                emptied_z = [0]
                empty_z_until(Z_KPE)
                square(z[:, Z_CQ:Z_CQ + 256], cn[:, 0:256], 1)
                square(z[:, Z_CQ + 256:Z_CQ + 384], cn[:, 256:384], 2)
                own.go(A.activation(values["diff"][:, t, :], z[:, Z_AV:Z_AV + GROUP], ACT.Copy), values_ready)
                empty_z_until(Z_DQ)
                own.link(A.activation(z[:, Z_U:Z_U + 512], z[:, Z_U:Z_U + 512], ACT.Gelu_apprx_tanh), gated)
                square(z[:, Z_V:Z_V + GROUP], squares[:, 0:GROUP], 3)
                empty_z_until(IN_W)
                own.go(A.activation(values["dil"][:, t, :], z[:, Z_DV:Z_DV + GROUP], ACT.Copy), values_ready)
                queries_keys("diff")
                exps("diff")
                own.go(A.activation(mq[:, :, :].rearrange("p h e -> p (h e)"), take("mq")[:, 0:HEADS * MQ], ACT.Copy), s_emptied)
                bank = take("mkv")[:, :].rearrange("p (h e) -> p h e", h=HEADS)
                own.go(A.activation(mk[:, :, 0:64], bank[:, :, 0:64], ACT.Copy), mk_ready)
                own.go(A.activation(values["mla"][:, t, :].rearrange("p (h e) -> p h e", h=HEADS), bank[:, :, 64:128], ACT.Copy), s_emptied)
                queries_keys("dil")
                exps("dil")
                turned("diff")
                for j, dst in enumerate((qT["mla"][0:MQ, :, :], kT["mla"][0:MQ, :, q_at])):
                    bank = take("mlaT", j)[0:MQ, :].rearrange("p (b q) -> p b q", b=4)
                    own.go(A.activation(dst, bank, ACT.Copy), s_emptied)
                exps("mla")
                turned("dil")
                turned("mla")
                act.wait_ge(mix_done, 1)
                for h in range(HEADS):
                    square(mix[:, 64 * h:64 * h + 64], scores[:, 0, 64 * h:64 * h + 64], 4 + h)
                for n in range(1, 4):
                    square(mix[:, GROUP * n:GROUP * (n + 1)], scores[:, 0, GROUP * n:GROUP * (n + 1)], 7 + n)
                act.wait_ge(x_ready, 1)
                square(x[:, t, :], scores[:, 0, 0:D], 11)
                gelu_dots()
                make_diags(2)
                for j in range(2):
                    bank = take("h2T", j)
                    own.go(A.activation(hT[:, 4 * j:4 * j + 4, :], bank[:, :].rearrange("p (k q) -> p k q", k=4), ACT.Copy), s_emptied)
                for j in range(2):
                    if j:
                        make_diags(1)
                    bank = take("peerq", j)
                    own.go(A.activation(peer_qT[:, 4 * j:4 * j + 4, :], bank[:, :].rearrange("p (h q) -> p h q", h=4), ACT.Copy), s_emptied)
                make_diags(1)
                by_half = key_scores.rearrange("p (h c) n -> p h c n", c=2)
                for j in range(4):
                    bank = take("keys", j)
                    h0 = j // 2 * 4
                    own.go(A.activation(by_half[:, h0:h0 + 4, j % 2, :], bank[:, :].rearrange("p (h n) -> p h n", h=4), ACT.Copy), s_emptied)
                make_diags(8)
                act.wait_ge(shifted, 1)
                own.go(A.activation(gate[:, t, :, :], gate[:, t, :, :], ACT.Exp), gates_exped)
                if gat:
                    make_diags(ROUNDS - made[0])

            def tensor_program(pe):
                summed = [0]
                finite_cols = mask_sb[:, :, :].rearrange("p m k -> p (m k)")[:, 0:CH]

                def sum_round(g):
                    for j, b in enumerate(PE_SLOTS):
                        pe.wait_ge(diag_made, g * HALF + (j + 1))
                        pe.wait_ge(row_loaded[b], (g_layer * (2 * T * ROUNDS) + g + (2 * gt + 1) * ROUNDS) * 16 + 16)
                        for c in range(2):
                            last = nc.tensor.matmul(pe_sum[c][:, :], diag[:, j, :], gathered[:, b, c * CH:(c + 1) * CH],
                                                    start=False, stop=False)
                        last.then_inc(pe_slots_free, 1)

                def sum_rows(n):
                    if gat:
                        if not summed[0]:
                            for c in range(2):
                                nc.tensor.matmul(pe_sum[c][:, :], zeros[:, :], finite_cols, start=True, stop=False)
                        rounds(pe, summed[0], n, sum_round)
                        summed[0] += n
                        if summed[0] == ROUNDS:
                            for c in range(2):
                                nc.tensor.matmul(pe_sum[c][:, :], zeros[:, :], finite_cols, start=False, stop=True).then_inc(pe_summed, 1)

                if not pre:
                    sum_rows(ROUNDS)
                    return
                counts = {"v": 0, "s": 0}

                def fill(side, *job):
                    n = counts[side]
                    jobs, emptied, bank = (V_JOBS, v_emptied, v_bank) if side == "v" else (S_JOBS, s_emptied, s_bank)
                    assert jobs[n] == job, (jobs[n], job)
                    counts[side] += 1
                    if n >= BANKS:
                        pe.wait_ge(emptied, n + 1 - BANKS)
                    return bank[n % BANKS]

                def v_done(*job):
                    pe.wait_ge(v_emptied, V_AT[job] + 1)

                def s_done(*job):
                    pe.wait_ge(s_emptied, S_AT[job] + 1)

                def transposes(bank, blocks, rows_out=P):
                    for n, b in enumerate(blocks):
                        last = nc.tensor.transpose(bank[0:rows_out, n * P:(n + 1) * P], b, id_sb[:, :])
                    return last

                def turn_wide(side, name, j):
                    bank = fill(side, name, j)
                    transposes(bank, [wide[:, t, k * P:(k + 1) * P] for k in range(4 * j, 4 * j + 4)])\
                        .then_inc(v_filled if side == "v" else s_filled, 1)

                pe.wait_ge(h_ready, 1)
                for j in range(2):
                    turn_wide("v", "hT", j)
                for c in range(NW):
                    pe.wait_ge(chunk_loaded[c % W_SLOTS], 16 * (c // W_SLOTS + 1))
                    bank = fill("s", "z", c)
                    v_done("hT", 1)
                    for k in range(KC):
                        last = nc.tensor.matmul(bank[:, 0:WC], hT[:, k, :], ring[:, c % W_SLOTS, k, :],
                                                start=(k == 0), stop=(k == KC - 1))
                    last.then_inc(s_filled, 1)

                def turn_heads(g, at):
                    pe.wait_ge(rotated[g], 1)
                    bank = fill("s", "qkT", g)
                    transposes(bank, [z[:, at + b * P:at + (b + 1) * P] for b in range(4)]).then_inc(s_filled, 1)

                def head_views(g, m):
                    if g == "mla":
                        return qT[g][0:MQ, m, :], kT[g][0:MQ, m, 0:kk]
                    w = P // ROW_TILES[g]
                    dims = slice(w * (m % ROW_TILES[g]), w * (m % ROW_TILES[g]) + w)
                    return qT[g][dims, m // ROW_TILES[g], :], kT[g][dims, m // ROW_TILES[g], 0:kk]

                def score(g):
                    for n, maps in enumerate(score_maps(g, t)):
                        bank = fill("v", "scores", g, n)
                        if n == 0:
                            s_done(*(("mlaT", 1) if g == "mla" else ("qkT", g)))
                        for i, m in enumerate(maps):
                            q, k = head_views(g, m)
                            last = nc.tensor.matmul(bank[:, i * kk:(i + 1) * kk], q, k, start=True, stop=True)
                        last.then_inc(v_filled, 1)

                def turn_and_weigh(g):
                    s = unit_view(g)
                    if g == "diff":
                        pe.wait_ge(combined, 1)
                    else:
                        pe.wait_ge(exped[g], MAPS[g])
                    blocks = [s[:, (2 * h if g == "diff" else h), k * P:(k + 1) * P] for h in range(HEADS) for k in range(t + 1)]
                    for n in range(t + 1):
                        bank = fill("s", "turn", g, n)
                        transposes(bank, blocks[4 * n:4 * n + 4]).then_inc(s_filled, 1)
                    bank = fill("v", "pv", g)
                    s_done("turn", g, t)
                    if g != "mla":
                        pe.wait_ge(values_ready, 1 if g == "diff" else 2)
                    for h in range(HEADS):
                        for k in range(t + 1):
                            at = (h * (t + 1) + k) * P
                            last = nc.tensor.matmul(bank[:, 64 * h:64 * h + 64], probsT[:, at:at + P],
                                                    values[g][:, k, 64 * h:64 * h + 64], start=(k == 0), stop=(k == t))
                    last.then_inc(v_filled, 1)

                turn_heads("diff", Z_AQ)
                score("diff")
                pe.wait_ge(latents_ready, 1)
                bank = fill("v", "cT")
                transposes(bank, [cn[:, j * P:(j + 1) * P] for j in range(3)]).then_inc(v_filled, 1)
                if t == 0:
                    pe.wait_ge(small_loaded, 7 * 16)
                bank = fill("s", "mq")
                v_done("cT")
                for j in range(2):
                    last = nc.tensor.matmul(bank[:, 0:HEADS * MQ], cT[:, j, :], uq_sb[:, j, :], start=(j == 0), stop=(j == 1))
                last.then_inc(s_filled, 1)
                bank = fill("s", "mkv")
                nc.tensor.matmul(bank[:, :], cT[:, 2, :], ukv_sb[:, :], start=True, stop=True).then_inc(s_filled, 1)
                turn_heads("dil", Z_DQ)
                score("dil")
                turn_and_weigh("diff")
                pe.wait_ge(rotated["mla"], 1)
                for j, src in enumerate((mq, mk)):
                    bank = fill("s", "mlaT", j)
                    transposes(bank, [src[:, h, :] for h in range(HEADS)], rows_out=MQ).then_inc(s_filled, 1)
                score("mla")
                turn_and_weigh("dil")
                bank = fill("v", "sgu")
                if t == 0:
                    pe.wait_ge(sgu_masked, 1)
                pe.wait_ge(gate_normed, 1)
                for g in range(4):
                    last = nc.tensor.matmul(bank[:, 64 * g:64 * g + 64], sgu_sb[:, g, :],
                                            z[:, Z_V + 64 * g:Z_V + 64 * g + 64], start=True, stop=True)
                last.then_inc(v_filled, 1)
                turn_and_weigh("mla")
                pe.wait_ge(mix_ready, 1)
                for j in range(2):
                    turn_wide("v", "mixT", j)
                for c in range(2):
                    if t == 0:
                        pe.wait_ge(kept_loaded[c], 16)
                    bank = fill("v", "proj", c)
                    v_done("mixT", 1)
                    for k in range(KC):
                        last = nc.tensor.matmul(bank[:, :], hT[:, k, :], w_kept[:, c, k, :], start=(k == 0), stop=(k == KC - 1))
                    last.then_inc(v_filled, 1)
                sum_rows(2)
                pe.wait_ge(h2_ready, 1)
                for j in range(2):
                    turn_wide("s", "h2T", j)
                for j in range(2):
                    if j:
                        sum_rows(1)
                    bank = fill("s", "peerq", j)
                    s_done("h2T", 1)
                    if t == 0:
                        pe.wait_ge(kept_loaded[2 + j], 16)
                    for i in range(4):
                        for k in range(KC):
                            last = nc.tensor.matmul(bank[:, i * P:(i + 1) * P], w_kept[:, 2 + j, k, i * P:(i + 1) * P], hT[:, k, :],
                                                    start=(k == 0), stop=(k == KC - 1))
                    last.then_inc(s_filled, 1)
                sum_rows(1)
                for j in range(4):
                    bank = fill("s", "keys", j)
                    s_done("peerq", j // 2)
                    for i in range(4):
                        h, half = j // 2 * 4 + i, j % 2
                        part = slice(64 * half, 64 * half + 64)
                        last = nc.tensor.matmul(bank[:, i * P:(i + 1) * P], peer_qT[part, h, :], keys_sb[part, :], start=True, stop=True)
                    last.then_inc(s_filled, 1)
                if gat:
                    sum_rows(ROUNDS - summed[0])

            def vector_program(dve):
                own = Counted(dve)
                V = nc.vector
                taken_jobs = []
                consumed = [0]

                def take(*job):
                    n = len(taken_jobs)
                    assert V_JOBS[n] == job, (V_JOBS[n], job)
                    taken_jobs.append(job)
                    dve.wait_ge(v_filled, n + 1)
                    return v_bank[n % BANKS]

                def dots_round(g):
                    for b in range(SLOTS):
                        dve.wait_ge(row_loaded[b], (g_layer * (2 * T * ROUNDS) + g + 2 * gt * ROUNDS) * 16 + 16)
                        V.scalar_tensor_tensor(gathered[:, b, :], gathered[:, b, :], 1.0, wide[:, gt, :], ALU.mult, ALU.mult,
                                               accum_out=dots[:, bass.ds(g * SLOTS + b, 1)]).then_inc(slots_free, 1)

                def sums_round(g):
                    for j, b in enumerate(DVE_SLOTS):
                        dve.wait_ge(slots_free, g * HALF + (SLOTS + PICKS + j))
                        dve.wait_ge(row_loaded[b], (g_layer * (2 * T * ROUNDS) + g + (2 * gt + 1) * ROUNDS) * 16 + 16)
                        V.scalar_tensor_tensor(x[:, gt, :], gathered[:, b, :], weights[:, bass.ds(g * SLOTS + b, 1)],
                                               x[:, gt, :], ALU.mult, ALU.add).then_inc(slots_free, 1)

                def weigh_gates():
                    dve.wait_ge(slots_free, SLOTS + PICKS)
                    own.link(V.tensor_copy(signal[:, 0:1], dots[:, 0:1]), dots_done)
                    dve.wait_ge(dots_gelud, 1)
                    own.link(V.tensor_tensor(weights[:, :], weights[:, :], gate[:, gt, :, :].rearrange("p h k -> p (h k)"), ALU.mult), weights_ready)

                def add_pe_sums():
                    dve.wait_ge(pe_summed, 2)
                    dve.wait_ge(slots_free, SLOTS + PICKS + PICKS // 2)
                    for c in range(2):
                        part = x[:, gt, c * CH:(c + 1) * CH]
                        own.link(V.tensor_tensor(part, part, pe_sum[c][:, :], ALU.add), vector_step)

                def consume(n):
                    if not gat:
                        return
                    first, last = consumed[0], consumed[0] + n
                    consumed[0] = last
                    assert last <= 2 * ROUNDS
                    if first < ROUNDS:
                        rounds(dve, first, min(last, ROUNDS) - first, dots_round)
                    if first < ROUNDS <= last:
                        at_middle()
                    if last > ROUNDS:
                        start = max(first, ROUNDS)
                        rounds(dve, start - ROUNDS, last - start, sums_round)

                at_middle = weigh_gates

                if not pre:
                    consume(2 * ROUNDS)
                    add_pe_sums()
                    return

                def mean(name, at, n, src, width, s):
                    first = POWERS[name][0] + at
                    own.link(V.tensor_scalar(ms[:, first:first + n], src, 1.0 / width, EPS, ALU.mult, ALU.add), s)

                def stat(name, at=0, n=1):
                    first = POWERS[name][0] + at
                    return rstd[:, first:first + n]

                def wait_rstd(name):
                    dve.wait_ge(rstd_ready, POWER_AT[name] + 1)

                dve.wait_ge(squared, 1)
                mean("mix_in", 0, 1, sumsq[:, 0:1], D, ms_ready)
                if t == 0:
                    dve.wait_ge(small_loaded, 7 * 16)
                    lv = row[:, R_LAM:NROW].rearrange("p (a b e) -> p a b e", a=2, b=2)
                    own.link(V.tensor_tensor(lam_prod[:, :, :], lv[:, :, 0, :], lv[:, :, 1, :], ALU.mult), vector_step)
                    own.link(V.tensor_reduce(lam_sum[:, :], lam_prod[:, :, :], AX, ALU.add), lam_summed)
                    own.link(V.tensor_scalar(col[:, C_OUT:C_OUT + 2], col[:, C_OUT:C_OUT + 2], lay[:, 1:2], None, ALU.mult), vector_step)
                    dve.wait_ge(lam_exped, 1)
                    own.link(V.tensor_tensor(lam[:, :], lam_exp[:, 0:1], lam_exp[:, 1:2], ALU.subtract), vector_step)
                    own.link(V.tensor_tensor(lam[:, :], lam[:, :], lay[:, 0:1], ALU.add), vector_step)
                consume(1)
                wait_rstd("mix_in")
                own.link(V.tensor_scalar(wide[:, t, :], x[:, t, :], stat("mix_in"), None, ALU.mult), h_ready)

                def empty_with_gain(bank, dst, gains, n):
                    own.link(V.tensor_tensor(dst, bank[:, 0:n * P].rearrange("p (k q) -> p k q", k=n), bc(gains, 2, P), ALU.mult), v_emptied)

                for j in range(2):
                    empty_with_gain(take("hT", j), hT[:, 4 * j:4 * j + 4, :], col[:, C_MIX + 4 * j:C_MIX + 4 * j + 4], 4)
                consume(5)
                dve.wait_ge(squared, 3)
                mean("latent", 0, 1, sumsq[:, 1:2], 256, vector_step)
                mean("latent", 1, 1, sumsq[:, 2:3], 128, ms_ready)
                consume(1)
                wait_rstd("latent")
                own.link(V.tensor_scalar(cn[:, 0:256], z[:, Z_CQ:Z_CQ + 256], stat("latent"), None, ALU.mult), vector_step)
                own.link(V.tensor_scalar(cn[:, 256:384], z[:, Z_CQ + 256:Z_CQ + 384], stat("latent", 1), None, ALU.mult), latents_ready)

                def mask(g):
                    s = unit_view(g)
                    m = mask_sb[:, 1 if g == "dil" else 0, t * P:t * P + kk]
                    by_row = s.rearrange("p (a r) k -> p a r k", r=ROW_TILES[g])
                    for n, maps in enumerate(score_maps(g, t)):
                        bank, per, a = take("scores", g, n), len(maps), maps[0] // ROW_TILES[g]
                        own.link(V.scalar_tensor_tensor(by_row[:, a:a + per, maps[0] % ROW_TILES[g], :],
                                                        bank[:, 0:per * kk].rearrange("p (m k) -> p m k", m=per), SCALE[g],
                                                        bc(m, 1, per), ALU.mult, ALU.add), v_emptied)
                    own.link(V.tensor_reduce(neg_max[g][:, :], s, AX, ALU.max, negate=True), masked)

                def normalise(g):
                    dve.wait_ge(exped[g], MAPS[g])
                    r = rden[g]
                    own.link(V.reciprocal(r[:, :], den[g][:, :]), vector_step)
                    if g != "diff":
                        return
                    second = r[:, :].rearrange("p (h m) -> p h m", m=2)[:, :, 1]
                    own.link(V.tensor_scalar(second, second, lam[:, 0:1], None, ALU.mult), vector_step)
                    s = unit_view(g)
                    for h in range(HEADS):
                        own.link(V.tensor_scalar(s[:, 2 * h + 1, :], s[:, 2 * h + 1, :], r[:, 2 * h + 1:2 * h + 2], None, ALU.mult), vector_step)
                    for h in range(HEADS):
                        own.link(V.scalar_tensor_tensor(s[:, 2 * h, :], s[:, 2 * h, :], r[:, 2 * h:2 * h + 1],
                                                        s[:, 2 * h + 1, :], ALU.mult, ALU.subtract),
                                 combined if h == HEADS - 1 else vector_step)

                def weighed(g):
                    bank = take("pv", g)
                    dst = mix[:, MIX_AT[g]:MIX_AT[g] + GROUP]
                    if g == "diff":
                        own.link(V.tensor_copy(dst, bank[:, 0:GROUP]), v_emptied)
                    else:
                        own.link(V.tensor_tensor(dst.rearrange("p (h e) -> p h e", h=HEADS),
                                                 bank[:, 0:GROUP].rearrange("p (h e) -> p h e", h=HEADS),
                                                 bc(rden[g][:, :], 2, 64), ALU.mult), v_emptied)

                consume(1)
                mask("diff")
                empty_with_gain(take("cT"), cT[:, :, :], col[:, C_QKV:C_QKV + 3], 3)
                dve.wait_ge(squared, 4)
                mean("gate", 0, 1, sumsq[:, 3:4], GROUP, ms_ready)
                consume(1)
                wait_rstd("gate")
                v = z[:, Z_V:Z_V + GROUP]
                own.link(V.scalar_tensor_tensor(v, v, stat("gate"), row[:, R_SGU:R_SGU + GROUP], ALU.mult, ALU.mult), gate_normed)
                mask("dil")
                normalise("diff")
                consume(1)
                weighed("diff")
                mask("mla")
                consume(1)
                normalise("dil")
                weighed("dil")
                bank = take("sgu")
                for g in range(4):
                    at = 64 * g
                    own.link(V.scalar_tensor_tensor(mix[:, 2 * GROUP + at:2 * GROUP + at + 64], bank[:, at:at + 64],
                                                    col[:, C_SGUB + g:C_SGUB + g + 1], z[:, Z_U + at:Z_U + at + 64],
                                                    ALU.add, ALU.mult), v_emptied if g == 3 else vector_step)
                consume(1)
                normalise("mla")
                weighed("mla")
                own.link(V.tensor_copy(signal[:, 1:2], sumsq[:, 0:1]), mix_done)
                consume(1)
                dve.wait_ge(squared, 11)
                mean("mixed", 0, 4, sumsq[:, 4:8], 64, vector_step)
                mean("mixed", 4, 3, sumsq[:, 8:11], GROUP, ms_ready)
                consume(1)
                wait_rstd("mixed")
                a = mix[:, 0:GROUP].rearrange("p (h e) -> p h e", h=HEADS)
                own.link(V.tensor_tensor(a, a, bc(stat("mixed", 0, 4), 2, 64), ALU.mult), vector_step)
                b = mix[:, GROUP:D].rearrange("p (h e) -> p h e", h=3)
                own.link(V.tensor_tensor(b, b, bc(stat("mixed", 4, 3), 2, GROUP), ALU.mult), mix_ready)
                for j in range(2):
                    empty_with_gain(take("mixT", j), hT[:, 4 * j:4 * j + 4, :], col[:, C_OUT + 4 * j:C_OUT + 4 * j + 4], 4)
                consume(1)
                for c in range(2):
                    bank = take("proj", c)
                    part = x[:, t, c * CH:(c + 1) * CH]
                    own.link(V.tensor_tensor(part, part, bank[:, :], ALU.add), v_emptied)
                own.link(V.tensor_copy(signal[:, 2:3], sumsq[:, 0:1]), x_ready)
                consume(1)
                dve.wait_ge(squared, 12)
                dve.wait_ge(ffn_loaded, 16)
                mean("ffn", 0, 1, sumsq[:, 11:12], D, ms_ready)
                consume(1)
                wait_rstd("ffn")
                own.link(V.scalar_tensor_tensor(wide[:, t, :], x[:, t, :], stat("ffn"), ffn_gain, ALU.mult, ALU.mult), h2_ready)
                consume(3)

                def top16(chains):
                    for step_ in range(5):
                        r = step_ // 3
                        for vals, numbers, src in chains:
                            part = slice(8 * r, 8 * r + 8)
                            if step_ in (0, 3):
                                ins = V.max(vals[:, part], src)
                            elif step_ in (1, 4):
                                ins = V.max_index(numbers[:, part], vals[:, part], src)
                            else:
                                ins = V.match_replace(src, vals[:, 0:8], src, LOWEST)
                            own.go(ins, vector_step)
                            dve.wait_ge(vector_step, own.value[id(vector_step)] - (len(chains) - 1))
                    dve.wait_ge(vector_step, own.value[id(vector_step)])

                for j in range(4):
                    dve.wait_ge(s_emptied, S_AT["keys", j // 2 * 2 + 1] + 1)
                    top16([(top_v[:, i, :], top_i[:, i, :], key_scores[:, i, :]) for i in range(4 * j, 4 * j + 4)])
                    consume(1)
                own.link(V.tensor_copy(top_f, top_i[:, :, :]), vector_step)
                tv = top_v.rearrange("p (h c) k -> p h c k", c=2)
                tf = top_f.rearrange("p (h c) k -> p h c k", c=2)
                own.link(V.tensor_tensor(pairs, bc(tv[:, :, 0, :], 3, TOPK), bc(tv[:, :, 1, :], 2, TOPK), ALU.add), vector_step)
                for j in range(4):
                    top16([(best[:, h, :], pos[:, h, :], pairs[:, h, :, :].rearrange("p i j -> p (i j)")) for h in range(2 * j, 2 * j + 2)])
                    if j == 3:
                        own.link(V.tensor_tensor(gate[:, t, :, :], best, best[:, :, 0:1].to_broadcast([P, PH, TOPK]), ALU.subtract), shifted)
                    consume(1)
                own.link(V.tensor_scalar(pos_hi, pos, 4, None, ALU.logical_shift_right), vector_step)
                own.link(V.tensor_copy(pos_hi_f, pos_hi), vector_step)
                own.link(V.tensor_scalar(pos, pos, TOPK - 1, None, ALU.bitwise_and), vector_step)
                own.link(V.tensor_copy(pos_f, pos), vector_step)
                hk = onehot.rearrange("p h k i -> p (h k) i")
                for c, which in enumerate((pos_hi_f, pos_f)):
                    w = which.rearrange("p h k -> p (h k)")
                    own.link(V.tensor_tensor(hk, bc(iota16[:, :], 1, PICKS), bc(w, 2, TOPK), ALU.is_equal), vector_step)
                    own.link(V.tensor_tensor(onehot, onehot, bc(tf[:, :, c, :], 2, TOPK), ALU.mult), vector_step)
                    own.link(V.tensor_reduce(key_of[:, c, :, :].rearrange("p h k -> p (h k)"), hk, AX, ALU.add), vector_step)
                    consume(1)
                k0 = key_of[:, 0, :, :].rearrange("p h k -> p (h k)")
                k1 = key_of[:, 1, :, :].rearrange("p h k -> p (h k)")
                own.link(V.scalar_tensor_tensor(expert_f, k0, float(NKEY), k1, ALU.mult, ALU.add), vector_step)
                own.link(V.tensor_scalar(expert[:, t, :], expert_f, lay[:, 2:3], None, ALU.add), vector_step)
                dve.wait_ge(gates_exped, 1)
                own.link(V.tensor_reduce(gate_sum[:, :], gate[:, t, :, :], AX, ALU.add), vector_step)
                own.link(V.reciprocal(gate_sum[:, :], gate_sum[:, :]), vector_step)
                own.link(V.tensor_tensor(gate[:, t, :, :], gate[:, t, :, :], bc(gate_sum[:, :], 2, TOPK), ALU.mult), vector_step)
                if gat:
                    consume(2 * ROUNDS - consumed[0])
                    add_pe_sums()

            def gpsimd_program(pool):
                own = Counted(pool)
                G = nc.gpsimd
                if gat:
                    G.sem_inc(slots_free, SLOTS)
                    G.sem_inc(pe_slots_free, HALF)
                issued = [0]

                def issue_until(last):
                    if not gat:
                        return
                    for half, table in enumerate((experts_u, experts_v)):
                        first = max(issued[0], half * ROUNDS)
                        n = min(last, (half + 1) * ROUNDS) - first

                        def gather_round(g, table=table, half=half):
                            for b in range(SLOTS):
                                n = g * SLOTS + (half * PICKS + b)
                                if half == 0:
                                    pool.wait_ge(slots_free, n + 1)
                                elif b in DVE_SLOTS:
                                    pool.wait_ge(slots_free, g * HALF + (SLOTS + PICKS - HALF + DVE_SLOTS.index(b) + 1))
                                else:
                                    pool.wait_ge(slots_free, PICKS + b + 1)
                                    pool.wait_ge(pe_slots_free, g * HALF + (PE_SLOTS.index(b) + 1))
                                G.sem_inc(gather_turn, 1)
                                G.tensor_copy(index_slot[:, b:b + 1], expert[:, gt, bass.ds(g * SLOTS + b, 1)]).then_inc(index_copied, 1)
                                pool.wait_ge(index_copied, n + 1)
                                G.sem_inc(gather_turn, 1)
                                G.indirect_dma_start(gathered[:, b, :], None, table,
                                                     bass.IndirectOffsetOnAxis(ap=index_slot[:, b:b + 1], axis=0)).then_inc(row_loaded[b], 16)

                        rounds(pool, first - half * ROUNDS, n, gather_round)
                    issued[0] = last

                if not pre:
                    issue_until(2 * ROUNDS)
                    return

                def power(name):
                    first, n = POWERS[name]
                    pool.wait_ge(ms_ready, POWER_AT[name] + 1)
                    own.link(G.tensor_tensor(rstd[:, first:first + n], ms[:, first:first + n], half_neg[:, 0:n], ALU.pow), rstd_ready)

                def rotate(view, n, half, at, done):
                    cos = bc(rope_sb[:, 0, t, at:at + half], 1, n)
                    sin = bc(rope_sb[:, 1, t, at:at + half], 1, n)
                    low, high = view[:, :, 0:half], view[:, :, half:2 * half]
                    part = [rot[:, i, 0:n * half].rearrange("p (n e) -> p n e", n=n) for i in range(4)]
                    own.go(G.tensor_tensor(part[0], low, cos, ALU.mult), gpsimd_step)
                    own.go(G.tensor_tensor(part[1], high, sin, ALU.mult), gpsimd_step)
                    own.go(G.tensor_tensor(part[2], high, cos, ALU.mult), gpsimd_step)
                    own.link(G.tensor_tensor(part[3], low, sin, ALU.mult), gpsimd_step)
                    own.go(G.tensor_tensor(low, part[0], part[1], ALU.subtract), gpsimd_step)
                    own.link(G.tensor_tensor(high, part[2], part[3], ALU.add), done)
                    pool.wait_ge(gpsimd_step, own.value[id(gpsimd_step)])

                issue_until(1)
                power("mix_in")
                if t == 0:
                    pool.wait_ge(small_loaded, 7 * 16)
                    own.link(G.tensor_tensor(sgu_sb[:, :, :], sgu_sb[:, :, :], bc(tri_sb[:, :], 1, 4), ALU.mult), sgu_masked)
                issue_until(4)
                pool.wait_ge(s_emptied, S_AT["z", z_chunk(Z_AV)] + 1)
                rotate(z[:, 0:512].rearrange("p (n e) -> p n e", e=32), 16, 4, 0, rotated["diff"])
                issue_until(7)
                power("latent")
                rotate(z[:, Z_KPE:Z_KPE + 32].rearrange("p (n e) -> p n e", n=1), 1, 16, 12, gpsimd_step)
                issue_until(8)
                pool.wait_ge(s_emptied, S_AT["z", NW - 1] + 1)
                rotate(z[:, Z_DQ:Z_DQ + 512].rearrange("p (n e) -> p n e", e=64), 8, 8, 4, rotated["dil"])
                issue_until(9)
                power("gate")
                pool.wait_ge(s_emptied, S_AT["mq",] + 1)
                rotate(mq[:, :, 64:MQ], HEADS, 16, 12, gpsimd_step)
                pool.wait_ge(mk_ready, 1)
                own.link(G.tensor_copy(mk[:, :, 64:MQ], bc(z[:, Z_KPE:Z_KPE + 32], 1, HEADS)), rotated["mla"])
                issue_until(14)
                power("mixed")
                issue_until(17)
                power("ffn")
                issue_until(2 * ROUNDS)

            with nc.Block() as block:
                @block.sync
                def _(sp):
                    sync_program(sp)

                @block.scalar
                def _(act):
                    scalar_program(act)

                @block.tensor
                def _(pe):
                    tensor_program(pe)

                @block.vector
                def _(dve):
                    vector_program(dve)

                @block.gpsimd
                def _(pool):
                    gpsimd_program(pool)

            for s in taken:
                nc.gpsimd.sem_clear(s)
            nc.all_engine_barrier()

        with nc.Block() as block:
            @block.sync
            def _(sp):
                sp.dma_start(x[:, :, :], x_in.rearrange("(t p) d -> p t d", p=P)).then_inc(const_loaded, 16)
                sp.dma_start(mask_sb[:, :, :], masks).then_inc(const_loaded, 16)
                sp.dma_start(rope_sb[:, :, :, :], rope).then_inc(const_loaded, 16)
                sp.dma_start(tri_sb[:, :], triangle).then_inc(const_loaded, 16)
                sp.dma_start(id_sb[:, :], identity).then_inc(const_loaded, 16)
                sp.wait_ge(const_loaded, 5 * 16)

            @block.gpsimd
            def _(pool):
                nc.gpsimd.memset(zeros[:, :], 0.0).then_inc(const_made, 1)
                nc.gpsimd.memset(half_neg[:, :], -0.5).then_inc(const_made, 1)
                nc.gpsimd.iota(iota16_i[:, :], [[1, TOPK]], base=0, channel_multiplier=0).then_inc(const_made, 1)
                pool.wait_ge(const_made, 3)
                nc.gpsimd.tensor_copy(iota16[:, :], iota16_i[:, :]).then_inc(const_made, 1)
                pool.wait_ge(const_made, 4)

        step((0, 0), None)
        with nc.Fori(0, L - 1) as layer:
            step((layer, 1), (layer, 0))
            step((layer + 1, 0), (layer, 1))
        step((L - 1, 1), (L - 1, 0))
        step(None, (L - 1, 1))

        final_sum, final_row = ctx.enter_context(nc.semaphore("final_sum")), ctx.enter_context(nc.semaphore("final_row"))
        final_ms, final_rstd = ctx.enter_context(nc.semaphore("final_ms")), ctx.enter_context(nc.semaphore("final_rstd"))
        final_out = ctx.enter_context(nc.semaphore("final_out"))
        first = POWERS["final"][0]
        with nc.Block() as block:
            @block.sync
            def _(sp):
                gain = final_gain.rearrange("(o n) -> o n", o=1).to_broadcast([P, D])
                sp.dma_start(z[:, 0:D], gain).then_inc(final_row, 16)
                for t in range(T):
                    sp.wait_ge(final_out, t + 1)
                    sp.dma_start(out[t * P:(t + 1) * P, :], wide[:, t, :]).then_inc(stored, 16)
                sp.wait_ge(stored, 16 * T)

            @block.scalar
            def _(act):
                for t in range(T):
                    nc.scalar.activation(gathered[:, t, :], x[:, t, :], ACT.Square, accum_out=sumsq[:, t:t + 1]).then_inc(final_sum, 1)

            @block.gpsimd
            def _(pool):
                pool.wait_ge(final_ms, 1)
                nc.gpsimd.tensor_tensor(rstd[:, first:first + T], ms[:, first:first + T], half_neg[:, 0:T], ALU.pow).then_inc(final_rstd, 1)

            @block.vector
            def _(dve):
                dve.wait_ge(final_sum, T)
                nc.vector.tensor_scalar(ms[:, first:first + T], sumsq[:, 0:T], 1.0 / D, EPS, ALU.mult, ALU.add).then_inc(final_ms, 1)
                dve.wait_ge(final_rstd, 1)
                dve.wait_ge(final_row, 16)
                for t in range(T):
                    nc.vector.scalar_tensor_tensor(wide[:, t, :], x[:, t, :], rstd[:, first + t:first + t + 1], z[:, 0:D],
                                                   ALU.mult, ALU.mult).then_inc(final_out, 1)


def shape_constants(seq):
    P, T = 128, seq // 128
    q = np.arange(seq)[:, None]
    k = np.arange(256)[None, :]
    causal = np.where(k <= q, 0.0, -1e30).astype(np.float32)
    count = np.zeros((seq, 256))
    for window, dil in ((128, 1), (512, 4), (2048, 16)):
        d = q - k
        count += (d >= 0) & (d % dil == 0) & (d // dil <= window // dil)
    dilated = np.where(count > 0, np.log(np.maximum(count, 1)), -1e30).astype(np.float32)
    masks = np.stack([causal, dilated]).reshape(2, T, P, 256).transpose(2, 0, 1, 3)
    masks = np.concatenate([masks[:, :, t, 0:P * (t + 1)] for t in range(T)], 2)
    angles = []
    for n_rot in (8, 16, 32):
        inv = np.float32(500000.0) ** (-np.arange(n_rot // 2, dtype=np.float32) * np.float32(2.0 / n_rot))
        angles.append(np.arange(seq, dtype=np.float32)[:, None] * inv[None, :])
    angles = np.concatenate(angles, 1).astype(np.float32)
    rope = np.stack([np.cos(angles), np.sin(angles)]).reshape(2, T, P, 28).transpose(2, 0, 1, 3)
    return {
        "masks": np.ascontiguousarray(masks), "rope": np.ascontiguousarray(rope),
        "triangle": np.triu(np.ones((P, P), np.float32)), "identity": np.eye(P, dtype=np.float32),
    }


def kernel(x, w_in, w_out, norm_mix, norm_ffn, diff_lambda, diff_head_norm, mla_q_norm, mla_kv_norm,
           mla_w_uq, mla_w_ukv, mla_out_norm, sgu_v_norm, sgu_w, sgu_b, sgu_out_norm, dil_out_norm,
           peer_w_q, peer_sub_keys, peer_u, peer_v, final_norm):
    import concourse.bacc as _bacc
    from concourse.bass_utils import run_bass_kernel_spmd as _run

    A = np.asarray
    L, seq, D = w_in.shape[0], x.shape[1], x.shape[2]
    n_experts = peer_u.shape[1]

    def down(a):
        a = A(a)
        return a.reshape(L, -1, 128).transpose(0, 2, 1)

    lam_init = [0.8 - 0.6 * math.exp(-0.3 * l) for l in range(L)]
    layer_consts = np.array([[v, 1.0 - v, l * n_experts] for l, v in enumerate(lam_init)], np.float32)
    arrays = {
        "x_in": A(x).reshape(seq, D), "w_in": A(w_in), "w_out": A(w_out), "w_q": A(peer_w_q),
        "columns": np.concatenate([down(norm_mix), down(mla_q_norm), down(mla_kv_norm), down(diff_head_norm),
                                   down(mla_out_norm), down(sgu_out_norm), down(dil_out_norm),
                                   A(sgu_b).transpose(0, 2, 1)], 2),
        "rows": np.concatenate([A(sgu_v_norm), A(diff_lambda).reshape(L, -1)], 1),
        "ffn_gains": A(norm_ffn),
        "layer_consts": np.repeat(layer_consts[:, None, :], 128, 1),
        "w_uq": A(mla_w_uq), "w_ukv": A(mla_w_ukv),
        "sgu_wt": A(sgu_w).transpose(0, 3, 1, 2), "keys_t": A(peer_sub_keys).transpose(0, 1, 3, 2).reshape(L, 128, -1),
        "experts_u": A(peer_u).reshape(L * n_experts, D), "experts_v": A(peer_v).reshape(L * n_experts, D),
        "final_gain": A(final_norm),
    }
    arrays.update(shape_constants(seq))
    nc = _bacc.Bacc("TRN2", target_bir_lowering=False, num_devices=1)
    feeds, args = {}, []
    for name, a in arrays.items():
        a = np.ascontiguousarray(a)
        feeds[f"in_{name}"] = a
        args.append(nc.dram_tensor(f"in_{name}", a.shape, mybir.dt.from_np(a.dtype), kind="ExternalInput").ap())
    args.append(nc.dram_tensor("out_0", (seq, D), mybir.dt.float32, kind="ExternalOutput").ap())
    bass_hybrid_trunk_peer(nc, *args)
    r = _run(nc, [feeds], core_ids=[0])
    return r.results[0]["out_0"].reshape(1, seq, D)
```

```python
import math
from contextlib import ExitStack

import numpy as np
import concourse.bass as bass
from concourse import mybir


def bass_hybrid_trunk_peer(
    nc: bass.Bass,
    x_in: bass.AP,
    w_in: bass.AP,
    w_out: bass.AP,
    w_q: bass.AP,
    columns: bass.AP,
    rows: bass.AP,
    ffn_gains: bass.AP,
    layer_consts: bass.AP,
    w_uq: bass.AP,
    w_ukv: bass.AP,
    sgu_wt: bass.AP,
    keys_t: bass.AP,
    experts_u: bass.AP,
    experts_v: bass.AP,
    final_gain: bass.AP,
    masks: bass.AP,
    rope: bass.AP,
    triangle: bass.AP,
    identity: bass.AP,
    out: bass.AP,
):
    fp32 = mybir.dt.float32
    u32 = mybir.dt.uint32
    ALU = mybir.AluOpType
    ACT = mybir.ActivationFunctionType
    AX = mybir.AxisListType.X

    P = 128
    L = w_in.shape[0]
    D = x_in.shape[1]
    T = x_in.shape[0] // P
    S = x_in.shape[0]
    KC = D // P
    IN_W = w_in.shape[2]
    CH = 512
    EPS = 1e-6
    GROUP = D // 4
    Z_AQ, Z_AV, Z_CQ, Z_KPE, Z_U, Z_V, Z_DQ, Z_DV = 0, 512, 768, 1152, 1184, 1440, 1696, 2208
    C_MIX, C_QKV, C_OUT, C_SGUB, NCOL = 0, 8, 11, 19, 23
    R_SGU, R_LAM, NROW = 0, GROUP, GROUP + 128
    HEADS = 4
    MQ = 96
    PH, TOPK, NKEY = 8, 16, 128
    PICKS = PH * TOPK
    SLOTS = 8
    ROUNDS = PICKS // SLOTS
    NW = 8
    WC = IN_W // NW
    W_SLOTS = 2
    LOWEST = -3.0e38
    PE_SLOTS = [4, 6, 7]
    DVE_SLOTS = [b for b in range(SLOTS) if b not in PE_SLOTS]
    NPE, NDVE = len(PE_SLOTS), len(DVE_SLOTS)
    AHEAD = ROUNDS // 2
    FIRST_ROWS = 3
    LATE = ROUNDS - AHEAD
    LATE_DOTS = LATE * SLOTS
    ALL_SUMS = LATE_DOTS + ROUNDS * NDVE
    BANKS = 3

    GROUPS = ("diff", "dil", "mla")
    MAPS = {"diff": 8, "dil": 4, "mla": 4}
    SCALE = {"diff": 32 ** -0.5, "dil": 64 ** -0.5, "mla": MQ ** -0.5}
    MIX_AT = {"diff": 0, "mla": GROUP, "dil": 3 * GROUP}
    ROW_TILES = {"diff": 4, "dil": 2, "mla": 1}

    def keys(t):
        return P * (t + 1)

    def score_maps(g, t):
        r, per = ROW_TILES[g], min(MAPS[g] // ROW_TILES[g], CH // keys(t))
        return [list(range(i + n * per * r, MAPS[g], r))[:per] for n in range(MAPS[g] // r // per) for i in range(r)]

    BETWEEN = {4: [("qkT", "diff")], 5: [("mq",), ("mkv",)]}


    def v_jobs(t):
        def of(g):
            return [("scores", g, n) for n in range(len(score_maps(g, t)))]
        jobs = [("cT",)] + of("diff") + of("dil") + [("pv", "diff")] + of("mla")
        jobs += [("pv", "dil"), ("sgu",), ("pv", "mla"), ("proj", 0), ("proj", 1)]
        return jobs

    def s_jobs(t, both, z_kept):
        def turn(g):
            return [("turn", g, n) for n in range(t + 1)]

        def more(*chunks):
            return [("next z", c) for c in chunks] if both else []
        jobs = [] if z_kept else [("hT", 0), ("hT", 1)]
        for c in range(NW):
            jobs += ([] if z_kept else [("z", c)]) + BETWEEN.get(c, [])
        if both:
            jobs += [("next hT", 0), ("next hT", 1)]
        jobs += [("qkT", "dil")] + more(0) + turn("diff")
        jobs += [("mlaT", 0), ("mlaT", 1)] + more(1) + turn("dil") + turn("mla") + more(2, 3)
        jobs += [("mixT", 0), ("mixT", 1)] + more(4) + [("h2T", 0), ("h2T", 1)]
        for j in range(2):
            jobs += [("peerq", j), ("keys", 2 * j), ("keys", 2 * j + 1)]
            if j == 0:
                jobs += more(*range(5, NW))
        return jobs

    POWERS = {"mix_in": (0, 1), "latent": (1, 2), "gate": (3, 1), "mixed": (4, 7), "ffn": (11, 1)}
    POWER_AT = {name: n for n, name in enumerate(POWERS)}

    ctx = ExitStack()
    with ctx:
        def sb(name, shape, dt=fp32):
            return ctx.enter_context(nc.sbuf_tensor(name, shape, dt))

        x = sb("x", [P, T, D])
        wide = sb("wide", [P, T, D])
        hT = sb("hT", [P, KC, P])
        z = sb("z", [P, IN_W])
        ring = sb("ring", [P, W_SLOTS, KC, WC])
        w_kept = sb("w_kept", [P, 4, KC, CH])
        gathered = sb("gathered", [P, SLOTS, D])
        scores = sb("scores", [P, 2, 8 * 256])
        qT = {"diff": sb("qT_diff", [P, 2, P]), "dil": sb("qT_dil", [P, 2, P]), "mla": sb("qT_mla", [P, 4, P])}
        kT = {"diff": sb("kT_diff", [P, 2, S]), "dil": sb("kT_dil", [P, 2, S]), "mla": sb("kT_mla", [P, 4, S])}
        values = {g: sb(f"values_{g}", [P, T, GROUP]) for g in GROUPS}
        mq = sb("mq", [P, HEADS, MQ])
        mk = sb("mk", [P, HEADS, MQ])
        cn = sb("cn", [P, 3 * P])
        cT = sb("cT", [P, 3, P])
        uq_sb = sb("uq_sb", [P, 2, HEADS * MQ])
        ukv_sb = sb("ukv_sb", [P, 512])
        sgu_sb = sb("sgu_sb", [P, 4, P])
        keys_sb = sb("keys_sb", [P, NKEY])
        col = sb("col", [P, NCOL])
        row = sb("row", [P, NROW])
        lay = sb("lay", [P, 3])
        mask_sb = sb("mask_sb", [P, 2, 3 * P])
        rope_sb = sb("rope_sb", [P, 2, T, 28])
        tri_sb = sb("tri_sb", [P, P])
        id_sb = sb("id_sb", [P, P])
        iota16 = sb("iota16", [P, TOPK])
        iota16_i = sb("iota16_i", [P, TOPK], mybir.dt.int32)
        half_neg = sb("half_neg", [P, 8])
        NEXT = 12
        ms = sb("ms", [P, 13])
        rstd = sb("rstd", [P, 13])
        sumsq = sb("sumsq", [P, 16])
        signal = sb("signal", [P, 4])
        rot = sb("rot", [P, 4, 64])
        neg_max = {g: sb(f"neg_max_{g}", [P, MAPS[g]]) for g in GROUPS}
        den = {g: sb(f"den_{g}", [P, MAPS[g]]) for g in GROUPS}
        rden = {g: sb(f"rden_{g}", [P, MAPS[g]]) for g in GROUPS}
        lam_prod = sb("lam_prod", [P, 2, 32])
        lam_sum = sb("lam_sum", [P, 2])
        lam_exp = sb("lam_exp", [P, 2])
        lam = sb("lam", [P, 1])
        top_i = sb("top_i", [P, 2 * PH, TOPK], u32)
        expert = sb("expert", [P, T, PICKS], u32)
        index_slot = sb("index_slot", [P, SLOTS], u32)
        gate = sb("gate", [P, T, PH, TOPK])
        gate_sum = sb("gate_sum", [P, PH])
        dots = sb("dots", [P, PICKS])
        weights = sb("weights", [P, PICKS])
        diag = sb("diag", [P, NPE, P])
        zeros = sb("zeros", [P, P])

        SPARE = SLOTS * D // (KC * WC)
        flat_gathered = gathered[:, :, :].rearrange("p b d -> p (b d)")
        next_hT = wide[:, 1, :].rearrange("p (k q) -> p k q", k=KC)
        z_next = ring[:, 0, :, :].rearrange("p k n -> p (k n)")
        spare = [flat_gathered[:, i * KC * WC:(i + 1) * KC * WC].rearrange("p (k n) -> p k n", k=KC) for i in range(SPARE)]
        squares = scores[:, 1, 0:D]
        score_of = {"diff": scores[:, 0, :], "dil": scores[:, 1, 0:D], "mla": scores[:, 1, D:2 * D]}
        probsT = z[:, 0:HEADS * T * P]
        ffn_gain = z[:, Z_V:Z_V + D]
        peer_qT = scores[:, 1, 0:D].rearrange("p (h q) -> p h q", h=PH)
        key_scores = z[:, 0:2 * PH * NKEY].rearrange("p (h n) -> p h n", n=NKEY)
        HALF_K = TOPK // 2
        PAIR_ROWS = TOPK + 1
        pairs = scores[:, 0, 0:PH // 2 * PAIR_ROWS * HALF_K].rearrange("p (h r j) -> p h r j", r=PAIR_ROWS, j=HALF_K)
        onehot = scores[:, 1, D:D + PH // 2 * TOPK * TOPK].rearrange("p (h k i) -> p h k i", k=TOPK, i=TOPK)
        top_f = cn[:, 0:2 * PH * TOPK].rearrange("p (h k) -> p h k", k=TOPK)
        flat_cT = cT[:, :, :].rearrange("p k q -> p (k q)")
        key_of = flat_cT[:, 0:2 * PICKS].rearrange("p (c h k) -> p c h k", c=2, k=TOPK)
        pos_f = flat_cT[:, 2 * PICKS:3 * PICKS].rearrange("p (h k) -> p h k", k=TOPK)
        top_v = rot[:, :, :].rearrange("p i (h k) -> p (i h) k", k=TOPK)
        flat_mk = mk[:, :, :].rearrange("p h e -> p (h e)")
        best = flat_mk[:, 0:PICKS].rearrange("p (h k) -> p h k", k=TOPK)
        pos = flat_mk[:, PICKS:2 * PICKS].bitcast(u32).rearrange("p (h k) -> p h k", k=TOPK)
        flat_mq = mq[:, :, :].rearrange("p h e -> p (h e)")
        pos_hi_f = flat_mq[:, 0:PICKS].rearrange("p (h k) -> p h k", k=TOPK)
        expert_f = flat_mq[:, PICKS:2 * PICKS]
        pos_hi = flat_mq[:, 2 * PICKS:3 * PICKS].bitcast(u32).rearrange("p (h k) -> p h k", k=TOPK)

        v_bank = [ctx.enter_context(nc.psum_tensor(f"v_bank{i}", [P, CH], fp32)) for i in range(BANKS)]
        s_bank = [ctx.enter_context(nc.psum_tensor(f"s_bank{i}", [P, CH], fp32)) for i in range(BANKS)]
        pe_sum = [ctx.enter_context(nc.psum_tensor(f"pe_sum{i}", [P, CH], fp32)) for i in range(2)]

        const_loaded = ctx.enter_context(nc.semaphore("const_loaded"))
        id_loaded = ctx.enter_context(nc.semaphore("id_loaded"))
        x_loaded = [ctx.enter_context(nc.semaphore(f"x_loaded{i}")) for i in range(T)]
        spare_loaded = [ctx.enter_context(nc.semaphore(f"spare_loaded{i}")) for i in range(SPARE)]
        const_made = ctx.enter_context(nc.semaphore("const_made"))
        stored = ctx.enter_context(nc.semaphore("stored"))
        head_loaded = [ctx.enter_context(nc.semaphore(f"head_loaded{i}")) for i in range(W_SLOTS)]
        row_loaded = [ctx.enter_context(nc.semaphore(f"row_loaded{i}")) for i in range(SLOTS)]

        def bc(ap, axis, n):
            a = ap.unsqueeze(axis)
            shape = list(a.shape)
            shape[axis] = n
            return a.to_broadcast(shape)

        class Counted:

            def __init__(self, eng):
                self.eng, self.value = eng, {}

            def go(self, ins, s, n=1):
                ins.then_inc(s, n)
                self.value[id(s)] = self.value.get(id(s), 0) + n

            def link(self, ins, s):
                self.go(ins, s)
                self.eng.wait_ge(s, self.value[id(s)])

        def rounds(eng, first, n, body):
            if n == 1:
                body(first)
            elif n > 1:
                with eng.Fori(first, first + n) as g:
                    body(g)

        def head_chunk(sp, c, layer):
            one = slice(layer, layer + 1) if isinstance(layer, int) else bass.ds(layer, 1)
            src = w_in[one].rearrange("o (k p) n -> p (o k) n", p=P)[:, :, c * WC:(c + 1) * WC]
            sp.dma_start(ring[:, c, :, :], src).then_inc(head_loaded[c], 16)

        issuer = {"sync": nc.sync, "scalar": nc.scalar, "tensor": nc.tensor, "vector": nc.vector, "gpsimd": nc.gpsimd}
        step_done = {name: ctx.enter_context(nc.semaphore(f"step_done_{name}")) for name in issuer}

        sets = [[], []]

        def steps_with(which_set):
            taken = sets[which_set]

            def sem(name):
                s = ctx.enter_context(nc.semaphore(f"{name}_{which_set}"))
                taken.append(s)
                return s

            small_loaded = sem("small_loaded")
            ffn_loaded = sem("ffn_loaded")
            next_loaded = [sem(f"next_loaded{i}") for i in range(1 + SPARE)]
            next_squared, next_ms, next_rstd, next_h = sem("next_squared"), sem("next_ms"), sem("next_rstd"), sem("next_h")
            chunk_loaded = [sem(f"chunk_loaded{i}") for i in range(W_SLOTS)]
            kept_loaded = [sem(f"kept_loaded{i}") for i in range(4)]
            v_filled, v_emptied = sem("v_filled"), sem("v_emptied")
            s_filled, s_emptied = sem("s_filled"), sem("s_emptied")
            final_gain_loaded, final_out = sem("final_gain_loaded"), sem("final_out")
            z_copied = sem("z_copied")
            squared = sem("squared")
            ms_ready = sem("ms_ready")
            rstd_ready = sem("rstd_ready")
            scalar_step = sem("scalar_step")
            vector_step = sem("vector_step")
            gpsimd_step = sem("gpsimd_step")
            values_ready = sem("values_ready")
            queries_turned = sem("queries_turned")
            mk_ready = sem("mk_ready")
            h_ready = sem("h_ready")
            latents_ready = sem("latents_ready")
            lam_summed = sem("lam_summed")
            lam_exped = sem("lam_exped")
            gated = sem("gated")
            gate_normed = sem("gate_normed")
            rotated = {g: sem(f"rotated_{g}") for g in GROUPS}
            sgu_masked = sem("sgu_masked")
            masked = sem("masked")
            exped = {g: sem(f"exped_{g}") for g in GROUPS}
            combined = sem("combined")
            mix_done = sem("mix_done")
            mix_ready = sem("mix_ready")
            x_ready = sem("x_ready")
            h2_ready = sem("h2_ready")
            experts_ready = sem("experts_ready")
            shifted = sem("shifted")
            gates_exped = sem("gates_exped")
            index_copied = sem("index_copied")
            gather_turn = sem("gather_turn")
            slots_free = sem("slots_free")
            pe_slots_free = sem("pe_slots_free")
            pe_summed = sem("pe_summed")
            diag_turn = sem("diag_turn")
            diag_made = sem("diag_made")
            weights_ready = sem("weights_ready")
            dots_done = sem("dots_done")
            dots_gelud = sem("dots_gelud")

            def step(name, eng, pre, gat, nxt):
                layer, t = pre if pre else (None, None)
                g_layer, gt = gat if gat else (None, None)
                both, z_kept = gat is None, pre == (0, 1)
                V_JOBS, S_JOBS = (v_jobs(t), s_jobs(t, both, z_kept)) if pre else ([], [])
                V_AT = {job: n for n, job in enumerate(V_JOBS)}
                S_AT = {job: n for n, job in enumerate(S_JOBS)}
                if pre:
                    one = slice(layer, layer + 1) if isinstance(layer, int) else bass.ds(layer, 1)
                    q_at, kk = slice(t * P, (t + 1) * P), keys(t)
                    mix = wide[:, t, :]

                def z_chunk(end):
                    return (end - 1) // WC

                def unit_view(g):
                    return score_of[g][:, 0:MAPS[g] * kk].rearrange("p (m k) -> p m k", m=MAPS[g])

                def power_at(name):
                    return POWER_AT[name] - (1 if z_kept else 0)

                def squares_by(n):
                    return n + (0 if z_kept else 1)

                def wait_z(eng, c):
                    if z_kept:
                        eng.wait_ge(z_copied, c + 1)
                    else:
                        eng.wait_ge(s_emptied, S_AT["z", c] + 1)

                def chunk_place(c):
                    if c < W_SLOTS:
                        steps = 1 if both else layer * T + t
                        return ring[:, c, :, :], head_loaded[c], steps * 16, None
                    n = W_SLOTS + (SPARE if both else 0)
                    if c % n >= W_SLOTS:
                        i = c % n - W_SLOTS
                        return spare[i], spare_loaded[i], 16 * (c // n + 1), (c - n if c >= n else None)
                    return ring[:, c % n, :, :], chunk_loaded[c % n], 16 * (c // n), c - n

                def next_place(c):
                    places = [ring[:, 1, :, :]] + spare
                    i, before = c % len(places), c - len(places)
                    last = max(k for k in range(NW) if k % (W_SLOTS + SPARE) == i + 1)
                    return places[i], next_loaded[i], 16 * (c // len(places) + 1), S_AT["next z", before] if before >= 0 else S_AT["z", last]

                def sync_program(sp):
                    for s in sets[1 - which_set]:
                        nc.sync.sem_clear(s)
                    if not pre:
                        sp.dma_start(z[:, 0:D], final_gain.rearrange("(o n) -> o n", o=1).to_broadcast([P, D])).then_inc(final_gain_loaded, 16)
                        for tile in range(T):
                            sp.wait_ge(final_out, tile + 1)
                            sp.dma_start(out[tile * P:(tile + 1) * P, :], wide[:, tile, :]).then_inc(stored, 16)
                        sp.wait_ge(stored, 16 * T)
                        return

                    if not gat:
                        for c in range(1, W_SLOTS):
                            head_chunk(sp, c, 0)
                        sp.dma_start(mask_sb[:, :, :], masks).then_inc(const_loaded, 16)
                        sp.dma_start(rope_sb[:, :, :, :], rope).then_inc(const_loaded, 16)
                        sp.dma_start(tri_sb[:, :], triangle).then_inc(const_loaded, 16)
                        for i in range(1, T):
                            sp.dma_start(x[:, i, :], x_in[i * P:(i + 1) * P, :]).then_inc(x_loaded[i], 16)
                    def w_in_chunk(c):
                        return w_in[one].rearrange("o (k p) n -> p (o k) n", p=P)[:, :, c * WC:(c + 1) * WC]

                    def next_chunk(c):
                        dst, loaded, _, last = next_place(c)
                        sp.wait_ge(s_filled, last + 1)
                        sp.dma_start(dst, w_in_chunk(c)).then_inc(loaded, 16)

                    for c in range(NW if z_kept else W_SLOTS, NW):
                        src = w_in_chunk(c)
                        dst, loaded, _, last = chunk_place(c)
                        if last is not None:
                            sp.wait_ge(s_filled, S_AT["z", last] + 1)
                        sp.dma_start(dst, src).then_inc(loaded, 16)
                    for c in range(4):
                        if both and c == 2:
                            for n in range(2):
                                next_chunk(n)
                        if t == 0:
                            w = (w_out if c < 2 else w_q)[one].rearrange("o (k p) n -> p (o k) n", p=P)
                            sp.dma_start(w_kept[:, c, :, :], w[:, :, c % 2 * CH:(c % 2 + 1) * CH]).then_inc(kept_loaded[c], 16)
                    if both:
                        for n in range(2, 6):
                            next_chunk(n)
                    sp.wait_ge(mix_done, 1)
                    sp.dma_start(ffn_gain, ffn_gains[one].to_broadcast([P, D])).then_inc(ffn_loaded, 16)
                    if both:
                        for c in range(6, NW):
                            next_chunk(c)
                        for i in range(1, T):
                            sp.wait_ge(x_loaded[i], 16)
                    elif nxt:
                        if z_kept:
                            wait_z(sp, NW - 1)
                        for c in range(W_SLOTS):
                            head_chunk(sp, c, nxt[0])

                def scalar_program(act):
                    own = Counted(act)
                    taken_jobs = []
                    A = nc.scalar

                    def take(*job):
                        n = len(taken_jobs)
                        assert S_JOBS[n] == job, (S_JOBS[n], job)
                        taken_jobs.append(job)
                        act.wait_ge(s_filled, n + 1)
                        return s_bank[n % BANKS]

                    def gelu_dots():
                        if gat:
                            act.wait_ge(dots_done, 1)
                            own.go(A.activation(weights[:, :], dots[:, :], ACT.Gelu_apprx_tanh), dots_gelud)

                    made = [0]

                    def diag_round(g):
                        for j, b in enumerate(PE_SLOTS):
                            act.wait_ge(pe_slots_free, g * NPE + (j + 1))
                            A.sem_inc(diag_turn, 1)
                            A.activation(diag[:, j, :], id_sb[:, :], ACT.Copy,
                                         scale=weights[:, bass.ds(g * SLOTS + b, 1)]).then_inc(diag_made, 1)

                    def make_diags(n):
                        if gat:
                            if not made[0]:
                                act.wait_ge(weights_ready, 1)
                            rounds(act, made[0], n, diag_round)
                            made[0] += n
                            assert made[0] <= ROUNDS

                    if not pre:
                        def final_squares(tile):
                            own.link(A.activation(scores[:, 0, 0:D], x[:, tile, :], ACT.Square, accum_out=sumsq[:, tile:tile + 1]), squared)

                        for tile in range(T - 1):
                            final_squares(tile)
                        gelu_dots()
                        make_diags(ROUNDS)
                        act.wait_ge(x_ready, 1)
                        final_squares(T - 1)
                        return
                    if t == 0:
                        act.dma_start(col[:, :], columns[one].rearrange("o p n -> p (o n)")).then_inc(small_loaded, 16)
                        act.dma_start(row[:, :], rows[one].to_broadcast([P, NROW])).then_inc(small_loaded, 16)
                        act.dma_start(lay[:, :], layer_consts[one].rearrange("o p n -> p (o n)")).then_inc(small_loaded, 16)
                        act.dma_start(uq_sb[:, :, :], w_uq[one].rearrange("o (k p) n -> p (o k) n", p=P)).then_inc(small_loaded, 16)
                        act.dma_start(ukv_sb[:, :], w_ukv[one].rearrange("o p n -> p (o n)")).then_inc(small_loaded, 16)
                        act.dma_start(sgu_sb[:, :, :], sgu_wt[one].rearrange("o s g t -> s (o g) t")).then_inc(small_loaded, 16)
                        act.dma_start(keys_sb[:, :], keys_t[one].rearrange("o p n -> p (o n)")).then_inc(small_loaded, 16)

                    def square(src, junk, at):
                        own.link(A.activation(junk, src, ACT.Square, accum_out=sumsq[:, at:at + 1]), squared)

                    if both:
                        act.wait_ge(x_loaded[0], 16)
                    if not z_kept:
                        square(x[:, t, :], squares, 0)

                    def turned_wide(name, gains):
                        for j in range(2):
                            bank = take(name, j)
                            for k in range(4 * j, 4 * j + 4):
                                ins = A.activation(hT[:, k, :], bank[:, k % 4 * P:(k % 4 + 1) * P], ACT.Copy,
                                                   scale=col[:, gains + k:gains + k + 1])
                                if k % 4 == 3:
                                    own.go(ins, s_emptied)

                    if not z_kept:
                        act.wait_ge(rstd_ready, power_at("mix_in") + 1)
                        own.go(A.activation(wide[:, t, :], x[:, t, :], ACT.Copy, scale=rstd[:, 0:1]), h_ready)
                    if t == 0:
                        act.wait_ge(small_loaded, 7 * 16)
                    if not z_kept:
                        turned_wide("hT", C_MIX)
                    if t == 0:
                        act.wait_ge(lam_summed, 1)
                        own.go(A.activation(lam_exp[:, :], lam_sum[:, :], ACT.Exp), lam_exped)

                    def exps(g):
                        act.wait_ge(masked, GROUPS.index(g) + 1)
                        s = unit_view(g)
                        for m in range(MAPS[g]):
                            own.go(A.activation(s[:, m, :], s[:, m, :], ACT.Exp, bias=neg_max[g][:, m:m + 1],
                                                accum_out=den[g][:, m:m + 1]), exped[g])

                    def turned(g):
                        flat = probsT[:, 0:HEADS * kk].rearrange("p (h k q) -> p h k q", h=HEADS, k=t + 1)
                        hn = 4 // (t + 1)
                        for n in range(t + 1):
                            bank = take("turn", g, n)
                            own.go(A.activation(flat[:, n * hn:(n + 1) * hn, :, :],
                                                bank[:, :].rearrange("p (h k q) -> p h k q", h=hn, k=t + 1), ACT.Copy), s_emptied)

                    def queries_keys(g):
                        bank = take("qkT", g)[:, :].rearrange("p (b q) -> p b q", b=4)
                        own.go(A.activation(qT[g][:, :, :], bank[:, 0:2, :], ACT.Copy), queries_turned)
                        own.go(A.activation(kT[g][:, :, q_at], bank[:, 2:4, :], ACT.Copy), s_emptied)

                    def empty_z_until(end):
                        for c in range(emptied_z[0], z_chunk(end) + 1):
                            cols = slice(c * WC, (c + 1) * WC)
                            if z_kept:
                                own.go(A.activation(z[:, cols], z_next[:, cols], ACT.Copy), z_copied)
                            else:
                                own.go(A.activation(z[:, cols], take("z", c)[:, 0:WC], ACT.Copy), s_emptied)
                        emptied_z[0] = z_chunk(end) + 1
                        wait_z(act, z_chunk(end))

                    def empty_next(*chunks):
                        if both:
                            for c in chunks:
                                bank = take("next z", c)
                                own.go(A.activation(z_next[:, c * WC:(c + 1) * WC], bank[:, 0:WC], ACT.Copy), s_emptied)

                    emptied_z = [0]
                    empty_z_until(Z_KPE)
                    square(z[:, Z_CQ:Z_CQ + 256], cn[:, 0:256], 1)
                    square(z[:, Z_CQ + 256:Z_CQ + 384], cn[:, 256:384], 2)
                    own.go(A.activation(values["diff"][:, t, :], z[:, Z_AV:Z_AV + GROUP], ACT.Copy), values_ready)
                    empty_z_until(5 * WC)
                    if both:
                        act.wait_ge(x_loaded[1], 16)
                        own.go(A.activation(squares, x[:, 1, :], ACT.Square, accum_out=sumsq[:, NEXT:NEXT + 1]), next_squared)
                        act.wait_ge(next_squared, 1)
                    queries_keys("diff")
                    empty_z_until(6 * WC)
                    own.link(A.activation(z[:, Z_U:Z_U + 512], z[:, Z_U:Z_U + 512], ACT.Gelu_apprx_tanh), gated)
                    square(z[:, Z_V:Z_V + GROUP], squares[:, 0:GROUP], 3)
                    own.go(A.activation(mq[:, :, :].rearrange("p h e -> p (h e)"), take("mq")[:, 0:HEADS * MQ], ACT.Copy), s_emptied)
                    bank = take("mkv")[:, :].rearrange("p (h e) -> p h e", h=HEADS)
                    own.go(A.activation(mk[:, :, 0:64], bank[:, :, 0:64], ACT.Copy), mk_ready)
                    own.go(A.activation(values["mla"][:, t, :].rearrange("p (h e) -> p h e", h=HEADS), bank[:, :, 64:128], ACT.Copy), s_emptied)
                    exps("diff")
                    if both:
                        act.wait_ge(next_rstd, 1)
                        own.go(A.activation(wide[:, 1, :], x[:, 1, :], ACT.Copy, scale=rstd[:, NEXT:NEXT + 1]), next_h)
                    empty_z_until(IN_W)
                    if both:
                        banks = [take("next hT", j) for j in range(2)]
                        for k in range(KC):
                            own.go(A.activation(next_hT[:, k, :], banks[k // 4][:, k % 4 * P:(k % 4 + 1) * P], ACT.Copy,
                                                scale=col[:, C_MIX + k:C_MIX + k + 1]), s_emptied if k % 4 == 3 else scalar_step)
                    own.go(A.activation(values["dil"][:, t, :], z[:, Z_DV:Z_DV + GROUP], ACT.Copy), values_ready)
                    gelu_dots()
                    make_diags(1)
                    queries_keys("dil")
                    exps("dil")
                    empty_next(0)
                    turned("diff")
                    make_diags(1)
                    for j, dst in enumerate((qT["mla"][0:MQ, :, :], kT["mla"][0:MQ, :, q_at])):
                        bank = take("mlaT", j)[0:MQ, :].rearrange("p (b q) -> p b q", b=4)
                        own.go(A.activation(dst, bank, ACT.Copy), s_emptied)
                    exps("mla")
                    empty_next(1)
                    turned("dil")
                    make_diags(1)
                    turned("mla")
                    make_diags(1)
                    act.wait_ge(mix_done, 1)
                    for h in range(HEADS):
                        square(mix[:, 64 * h:64 * h + 64], scores[:, 0, 64 * h:64 * h + 64], 4 + h)
                    for n in range(1, 4):
                        square(mix[:, GROUP * n:GROUP * (n + 1)], scores[:, 0, GROUP * n:GROUP * (n + 1)], 7 + n)
                    make_diags(1)
                    empty_next(2, 3)
                    turned_wide("mixT", C_OUT)
                    make_diags(2)
                    act.wait_ge(x_ready, 1)
                    square(x[:, t, :], scores[:, 0, 0:D], 11)
                    make_diags(1)
                    empty_next(4)
                    for j in range(2):
                        bank = take("h2T", j)
                        own.go(A.activation(hT[:, 4 * j:4 * j + 4, :], bank[:, :].rearrange("p (k q) -> p k q", k=4), ACT.Copy), s_emptied)
                    make_diags(2)
                    by_half = key_scores.rearrange("p (h c) n -> p h c n", c=2)
                    for j in range(2):
                        bank = take("peerq", j)
                        own.go(A.activation(peer_qT[:, 4 * j:4 * j + 4, :], bank[:, :].rearrange("p (h q) -> p h q", h=4), ACT.Copy), s_emptied)
                        for c in range(2):
                            bank = take("keys", 2 * j + c)
                            own.go(A.activation(by_half[:, 4 * j:4 * j + 4, c, :], bank[:, :].rearrange("p (h n) -> p h n", h=4), ACT.Copy), s_emptied)
                        if j == 0:
                            empty_next(*range(5, NW))
                            make_diags(ROUNDS - made[0])
                    act.wait_ge(shifted, 1)
                    own.go(A.activation(gate[:, t, :, :], gate[:, t, :, :], ACT.Exp), gates_exped)

                def tensor_program(pe):
                    summed = [0]
                    finite_cols = mask_sb[:, :, :].rearrange("p m k -> p (m k)")[:, 0:CH]

                    def sum_round(g, closing=False):
                        for j, b in enumerate(PE_SLOTS):
                            pe.wait_ge(diag_made, g * NPE + (j + 1))
                            pe.wait_ge(row_loaded[b], (g_layer * (2 * T * ROUNDS) + g + (2 * gt + 1) * ROUNDS) * 16 + 16)
                            ends = closing and j == NPE - 1
                            for c in range(2):
                                last = nc.tensor.matmul(pe_sum[c][:, :], diag[:, j, :], gathered[:, b, c * CH:(c + 1) * CH],
                                                        start=False, stop=ends)
                                if ends:
                                    last.then_inc(pe_summed, 1)
                            if not ends:
                                last.then_inc(pe_slots_free, 1)

                    def sum_rows(n):
                        if gat:
                            if not summed[0]:
                                for c in range(2):
                                    nc.tensor.matmul(pe_sum[c][:, :], zeros[:, :], finite_cols, start=True, stop=False)
                            first = summed[0]
                            summed[0] += n
                            closing = summed[0] == ROUNDS
                            rounds(pe, first, n - 1 if closing else n, sum_round)
                            if closing:
                                sum_round(ROUNDS - 1, True)

                    if not pre:
                        sum_rows(ROUNDS)
                        return
                    counts = {"v": 0, "s": 0}

                    def fill(side, *job):
                        n = counts[side]
                        jobs, emptied, bank = (V_JOBS, v_emptied, v_bank) if side == "v" else (S_JOBS, s_emptied, s_bank)
                        assert jobs[n] == job, (jobs[n], job)
                        counts[side] += 1
                        if n >= BANKS:
                            pe.wait_ge(emptied, n + 1 - BANKS)
                        return bank[n % BANKS]

                    def v_done(*job):
                        pe.wait_ge(v_emptied, V_AT[job] + 1)

                    def s_done(*job):
                        pe.wait_ge(s_emptied, S_AT[job] + 1)

                    def transposes(bank, blocks, rows_out=P):
                        for n, b in enumerate(blocks):
                            last = nc.tensor.transpose(bank[0:rows_out, n * P:(n + 1) * P], b, id_sb[:, :])
                        return last

                    def turn_wide(name, j, tile=t):
                        bank = fill("s", name, j)
                        transposes(bank, [wide[:, tile, k * P:(k + 1) * P] for k in range(4 * j, 4 * j + 4)])\
                            .then_inc(s_filled, 1)

                    if not gat:
                        pe.wait_ge(id_loaded, 16)
                    if not z_kept:
                        pe.wait_ge(h_ready, 1)
                        for j in range(2):
                            turn_wide("hT", j)
                    def turn_heads(g, at):
                        pe.wait_ge(rotated[g], 1)
                        bank = fill("s", "qkT", g)
                        transposes(bank, [z[:, at + b * P:at + (b + 1) * P] for b in range(4)]).then_inc(s_filled, 1)

                    def head_views(g, m):
                        if g == "mla":
                            return qT[g][0:MQ, m, :], kT[g][0:MQ, m, 0:kk]
                        w = P // ROW_TILES[g]
                        dims = slice(w * (m % ROW_TILES[g]), w * (m % ROW_TILES[g]) + w)
                        return qT[g][dims, m // ROW_TILES[g], :], kT[g][dims, m // ROW_TILES[g], 0:kk]

                    def score(g):
                        for n, maps in enumerate(score_maps(g, t)):
                            bank = fill("v", "scores", g, n)
                            if n == 0:
                                s_done(*(("mlaT", 1) if g == "mla" else ("qkT", g)))
                            for i, m in enumerate(maps):
                                q, k = head_views(g, m)
                                last = nc.tensor.matmul(bank[:, i * kk:(i + 1) * kk], q, k, start=True, stop=True)
                            last.then_inc(v_filled, 1)

                    def turn_and_weigh(g):
                        s = unit_view(g)
                        if g == "diff":
                            pe.wait_ge(combined, 1)
                        else:
                            pe.wait_ge(exped[g], MAPS[g])
                        blocks = [s[:, (2 * h if g == "diff" else h), k * P:(k + 1) * P] for h in range(HEADS) for k in range(t + 1)]
                        for n in range(t + 1):
                            bank = fill("s", "turn", g, n)
                            transposes(bank, blocks[4 * n:4 * n + 4]).then_inc(s_filled, 1)
                        bank = fill("v", "pv", g)
                        s_done("turn", g, t)
                        if g != "mla":
                            pe.wait_ge(values_ready, 1 if g == "diff" else 2)
                        for h in range(HEADS):
                            for k in range(t + 1):
                                at = (h * (t + 1) + k) * P
                                last = nc.tensor.matmul(bank[:, 64 * h:64 * h + 64], probsT[:, at:at + P],
                                                        values[g][:, k, 64 * h:64 * h + 64], start=(k == 0), stop=(k == t))
                        last.then_inc(v_filled, 1)

                    def z_chunk_of(bank, chunk, left):
                        for k in range(KC):
                            last = nc.tensor.matmul(bank[:, 0:WC], left[:, k, :], chunk[:, k, :], start=(k == 0), stop=(k == KC - 1))
                        last.then_inc(s_filled, 1)

                    def next_z(*chunks):
                        if both:
                            for c in chunks:
                                chunk, loaded, value, _ = next_place(c)
                                pe.wait_ge(loaded, value)
                                bank = fill("s", "next z", c)
                                s_done("next hT", 1)
                                z_chunk_of(bank, chunk, next_hT)

                    for c in range(NW):
                        if not z_kept:
                            chunk, loaded, value, _ = chunk_place(c)
                            pe.wait_ge(loaded, value)
                            bank = fill("s", "z", c)
                            s_done("hT", 1)
                            z_chunk_of(bank, chunk, hT)
                        if c == 4:
                            turn_heads("diff", Z_AQ)
                        elif c == 5:
                            pe.wait_ge(latents_ready, 1)
                            transposes(fill("v", "cT"), [cn[:, j * P:(j + 1) * P] for j in range(3)]).then_inc(v_filled, 1)
                            if t == 0:
                                pe.wait_ge(small_loaded, 7 * 16)
                            bank = fill("s", "mq")
                            v_done("cT")
                            for j in range(2):
                                last = nc.tensor.matmul(bank[:, 0:HEADS * MQ], cT[:, j, :], uq_sb[:, j, :], start=(j == 0), stop=(j == 1))
                            last.then_inc(s_filled, 1)
                            bank = fill("s", "mkv")
                            nc.tensor.matmul(bank[:, :], cT[:, 2, :], ukv_sb[:, :], start=True, stop=True).then_inc(s_filled, 1)
                            score("diff")
                    if both:
                        pe.wait_ge(next_h, 1)
                        for j in range(2):
                            turn_wide("next hT", j, 1)
                    turn_heads("dil", Z_DQ)
                    score("dil")
                    next_z(0)
                    sum_rows(1)
                    turn_and_weigh("diff")
                    pe.wait_ge(rotated["mla"], 1)
                    for j, src in enumerate((mq, mk)):
                        bank = fill("s", "mlaT", j)
                        transposes(bank, [src[:, h, :] for h in range(HEADS)], rows_out=MQ).then_inc(s_filled, 1)
                    score("mla")
                    next_z(1)
                    sum_rows(1)
                    turn_and_weigh("dil")
                    bank = fill("v", "sgu")
                    if t == 0:
                        pe.wait_ge(sgu_masked, 1)
                    pe.wait_ge(gate_normed, 1)
                    for g in range(4):
                        last = nc.tensor.matmul(bank[:, 64 * g:64 * g + 64], sgu_sb[:, g, :],
                                                z[:, Z_V + 64 * g:Z_V + 64 * g + 64], start=True, stop=True)
                    last.then_inc(v_filled, 1)
                    sum_rows(1)
                    turn_and_weigh("mla")
                    next_z(2, 3)
                    sum_rows(2)
                    pe.wait_ge(mix_ready, 1)
                    for j in range(2):
                        turn_wide("mixT", j)
                    for c in range(2):
                        if t == 0:
                            pe.wait_ge(kept_loaded[c], 16)
                        bank = fill("v", "proj", c)
                        s_done("mixT", 1)
                        for k in range(KC):
                            last = nc.tensor.matmul(bank[:, :], hT[:, k, :], w_kept[:, c, k, :], start=(k == 0), stop=(k == KC - 1))
                        last.then_inc(v_filled, 1)
                        sum_rows(1)
                    sum_rows(1)
                    next_z(4)
                    pe.wait_ge(h2_ready, 1)
                    for j in range(2):
                        turn_wide("h2T", j)
                    for j in range(2):
                        bank = fill("s", "peerq", j)
                        s_done("h2T", 1)
                        if t == 0:
                            pe.wait_ge(kept_loaded[2 + j], 16)
                        for i in range(4):
                            for k in range(KC):
                                last = nc.tensor.matmul(bank[:, i * P:(i + 1) * P], w_kept[:, 2 + j, k, i * P:(i + 1) * P], hT[:, k, :],
                                                        start=(k == 0), stop=(k == KC - 1))
                            if i == 3:
                                last.then_inc(s_filled, 1)
                            if j == 0 and i % 2:
                                sum_rows(1)
                        for c in range(2):
                            bank = fill("s", "keys", 2 * j + c)
                            s_done("peerq", j)
                            part = slice(64 * c, 64 * c + 64)
                            for i in range(4):
                                last = nc.tensor.matmul(bank[:, i * P:(i + 1) * P], peer_qT[part, 4 * j + i, :], keys_sb[part, :],
                                                        start=True, stop=True)
                            last.then_inc(s_filled, 1)
                        if j == 0:
                            next_z(*range(5, NW))
                            if gat:
                                sum_rows(ROUNDS - summed[0])

                def vector_program(dve):
                    own = Counted(dve)
                    V = nc.vector
                    taken_jobs = []
                    consumed = [0]

                    def take(*job):
                        n = len(taken_jobs)
                        assert V_JOBS[n] == job, (V_JOBS[n], job)
                        taken_jobs.append(job)
                        dve.wait_ge(v_filled, n + 1)
                        return v_bank[n % BANKS]

                    def dots_of(tile_layer, tile):
                        def dots_round(g, slots=range(SLOTS)):
                            for b in slots:
                                dve.wait_ge(row_loaded[b], (tile_layer * (2 * T * ROUNDS) + g + 2 * tile * ROUNDS) * 16 + 16)
                                V.scalar_tensor_tensor(gathered[:, b, :], gathered[:, b, :], 1.0, wide[:, tile, :], ALU.mult, ALU.mult,
                                                       accum_out=dots[:, bass.ds(g * SLOTS + b, 1)]).then_inc(slots_free, 1)
                        return dots_round

                    def sums_round(g):
                        for j, b in enumerate(DVE_SLOTS):
                            dve.wait_ge(slots_free, g * NDVE + (LATE_DOTS + j))
                            dve.wait_ge(row_loaded[b], (g_layer * (2 * T * ROUNDS) + g + (2 * gt + 1) * ROUNDS) * 16 + 16)
                            V.scalar_tensor_tensor(x[:, gt, :], gathered[:, b, :], weights[:, bass.ds(g * SLOTS + b, 1)],
                                                   x[:, gt, :], ALU.mult, ALU.add).then_inc(slots_free, 1)

                    def weigh_gates():
                        dve.wait_ge(slots_free, LATE_DOTS)
                        own.link(V.tensor_copy(signal[:, 0:1], dots[:, 0:1]), dots_done)
                        gates = gate[:, gt, :, :]
                        own.link(V.tensor_reduce(gate_sum[:, :], gates, AX, ALU.add), vector_step)
                        own.link(V.reciprocal(gate_sum[:, :], gate_sum[:, :]), vector_step)
                        own.link(V.tensor_tensor(gates, gates, bc(gate_sum[:, :], 2, TOPK), ALU.mult), vector_step)
                        dve.wait_ge(dots_gelud, 1)
                        own.link(V.tensor_tensor(weights[:, :], weights[:, :], gate[:, gt, :, :].rearrange("p h k -> p (h k)"), ALU.mult), weights_ready)

                    def add_pe_sums():
                        if gat:
                            dve.wait_ge(pe_summed, 2)
                            dve.wait_ge(slots_free, ALL_SUMS)
                            for c in range(2):
                                part = x[:, gt, c * CH:(c + 1) * CH]
                                own.link(V.tensor_tensor(part, part, pe_sum[c][:, :], ALU.add), vector_step)

                    def consume(n):
                        if not gat:
                            return
                        first, last = consumed[0], consumed[0] + n
                        consumed[0] = last
                        assert last <= LATE + ROUNDS
                        if first < LATE:
                            rounds(dve, first + AHEAD, min(last, LATE) - first, dots_of(g_layer, gt))
                        if first < LATE <= last:
                            weigh_gates()
                        if last > LATE:
                            start = max(first, LATE)
                            rounds(dve, start - LATE, last - start, sums_round)

                    def look_ahead(n):
                        rounds(dve, ahead[0], n, dots_of(layer, t))
                        ahead[0] += n

                    ahead = [0]
                    if not pre:
                        def final_mean(tile):
                            dve.wait_ge(squared, tile + 1)
                            own.link(V.tensor_scalar(ms[:, tile:tile + 1], sumsq[:, tile:tile + 1], 1.0 / D, EPS, ALU.mult, ALU.add), ms_ready)

                        def final_norm(tile):
                            dve.wait_ge(rstd_ready, tile + 1)
                            own.link(V.scalar_tensor_tensor(wide[:, tile, :], x[:, tile, :], rstd[:, tile:tile + 1], z[:, 0:D],
                                                            ALU.mult, ALU.mult), final_out)

                        consume(1)
                        for tile in range(T - 1):
                            final_mean(tile)
                        consume(1)
                        dve.wait_ge(final_gain_loaded, 16)
                        for tile in range(T - 1):
                            final_norm(tile)
                        consume(LATE + ROUNDS - 2)
                        add_pe_sums()
                        own.link(V.tensor_copy(signal[:, 2:3], ms[:, 0:1]), x_ready)
                        final_mean(T - 1)
                        final_norm(T - 1)
                        return

                    def mean(name, at, n, src, width, s):
                        first = POWERS[name][0] + at
                        own.link(V.tensor_scalar(ms[:, first:first + n], src, 1.0 / width, EPS, ALU.mult, ALU.add), s)

                    def stat(name, at=0, n=1):
                        first = POWERS[name][0] + at
                        return rstd[:, first:first + n]

                    def wait_rstd(name):
                        dve.wait_ge(rstd_ready, power_at(name) + 1)

                    if gat:
                        dots_of(g_layer, gt)(AHEAD, range(FIRST_ROWS))
                    if not z_kept:
                        dve.wait_ge(squared, squares_by(0))
                        mean("mix_in", 0, 1, sumsq[:, 0:1], D, ms_ready)
                    if gat:
                        dots_of(g_layer, gt)(AHEAD, range(FIRST_ROWS, SLOTS))
                        consumed[0] = 1
                    if t == 0:
                        dve.wait_ge(small_loaded, 7 * 16)
                        lv = row[:, R_LAM:NROW].rearrange("p (a b e) -> p a b e", a=2, b=2)
                        own.link(V.tensor_tensor(lam_prod[:, :, :], lv[:, :, 0, :], lv[:, :, 1, :], ALU.mult), vector_step)
                        own.link(V.tensor_reduce(lam_sum[:, :], lam_prod[:, :, :], AX, ALU.add), lam_summed)
                        own.link(V.tensor_scalar(col[:, C_OUT:C_OUT + 2], col[:, C_OUT:C_OUT + 2], lay[:, 1:2], None, ALU.mult), vector_step)
                        dve.wait_ge(lam_exped, 1)
                        own.link(V.tensor_tensor(lam[:, :], lam_exp[:, 0:1], lam_exp[:, 1:2], ALU.subtract), vector_step)
                        own.link(V.tensor_tensor(lam[:, :], lam[:, :], lay[:, 0:1], ALU.add), vector_step)
                    def empty_with_gain(bank, dst, gains, n):
                        own.link(V.tensor_tensor(dst, bank[:, 0:n * P].rearrange("p (k q) -> p k q", k=n), bc(gains, 2, P), ALU.mult), v_emptied)

                    consume(2)
                    dve.wait_ge(squared, squares_by(2))
                    mean("latent", 0, 1, sumsq[:, 1:2], 256, vector_step)
                    mean("latent", 1, 1, sumsq[:, 2:3], 128, ms_ready)
                    consume(1)
                    wait_rstd("latent")
                    own.link(V.tensor_scalar(cn[:, 0:256], z[:, Z_CQ:Z_CQ + 256], stat("latent"), None, ALU.mult), vector_step)
                    own.link(V.tensor_scalar(cn[:, 256:384], z[:, Z_CQ + 256:Z_CQ + 384], stat("latent", 1), None, ALU.mult), latents_ready)

                    def mask(g):
                        s = unit_view(g)
                        m = mask_sb[:, 1 if g == "dil" else 0, t * P:t * P + kk]
                        by_row = s.rearrange("p (a r) k -> p a r k", r=ROW_TILES[g])
                        for n, maps in enumerate(score_maps(g, t)):
                            bank, per, a = take("scores", g, n), len(maps), maps[0] // ROW_TILES[g]
                            own.link(V.scalar_tensor_tensor(by_row[:, a:a + per, maps[0] % ROW_TILES[g], :],
                                                            bank[:, 0:per * kk].rearrange("p (m k) -> p m k", m=per), SCALE[g],
                                                            bc(m, 1, per), ALU.mult, ALU.add), v_emptied)
                        own.link(V.tensor_reduce(neg_max[g][:, :], s, AX, ALU.max, negate=True), masked)

                    def normalise(g):
                        dve.wait_ge(exped[g], MAPS[g])
                        r = rden[g]
                        own.link(V.reciprocal(r[:, :], den[g][:, :]), vector_step)
                        if g != "diff":
                            return
                        second = r[:, :].rearrange("p (h m) -> p h m", m=2)[:, :, 1]
                        own.link(V.tensor_scalar(second, second, lam[:, 0:1], None, ALU.mult), vector_step)
                        s = unit_view(g)
                        for h in range(HEADS):
                            own.link(V.tensor_scalar(s[:, 2 * h + 1, :], s[:, 2 * h + 1, :], r[:, 2 * h + 1:2 * h + 2], None, ALU.mult), vector_step)
                        for h in range(HEADS):
                            own.link(V.scalar_tensor_tensor(s[:, 2 * h, :], s[:, 2 * h, :], r[:, 2 * h:2 * h + 1],
                                                            s[:, 2 * h + 1, :], ALU.mult, ALU.subtract),
                                     combined if h == HEADS - 1 else vector_step)

                    def weighed(g):
                        bank = take("pv", g)
                        dst = mix[:, MIX_AT[g]:MIX_AT[g] + GROUP]
                        if g == "diff":
                            own.link(V.tensor_copy(dst, bank[:, 0:GROUP]), v_emptied)
                        else:
                            own.link(V.tensor_tensor(dst.rearrange("p (h e) -> p h e", h=HEADS),
                                                     bank[:, 0:GROUP].rearrange("p (h e) -> p h e", h=HEADS),
                                                     bc(rden[g][:, :], 2, 64), ALU.mult), v_emptied)

                    empty_with_gain(take("cT"), cT[:, :, :], col[:, C_QKV:C_QKV + 3], 3)
                    consume(1)
                    if not gat:
                        dve.wait_ge(const_loaded, 3 * 16)
                    mask("diff")
                    consume(1)
                    if both:
                        dve.wait_ge(next_squared, 1)
                        own.link(V.tensor_scalar(ms[:, NEXT:NEXT + 1], sumsq[:, NEXT:NEXT + 1], 1.0 / D, EPS, ALU.mult, ALU.add), next_ms)
                    dve.wait_ge(squared, squares_by(3))
                    mean("gate", 0, 1, sumsq[:, 3:4], GROUP, ms_ready)
                    consume(1)
                    wait_rstd("gate")
                    v = z[:, Z_V:Z_V + GROUP]
                    own.link(V.scalar_tensor_tensor(v, v, stat("gate"), row[:, R_SGU:R_SGU + GROUP], ALU.mult, ALU.mult), gate_normed)
                    normalise("diff")
                    consume(2)
                    mask("dil")
                    consume(1)
                    weighed("diff")
                    mask("mla")
                    consume(1)
                    normalise("dil")
                    weighed("dil")
                    bank = take("sgu")
                    for g in range(4):
                        at = 64 * g
                        own.link(V.scalar_tensor_tensor(mix[:, 2 * GROUP + at:2 * GROUP + at + 64], bank[:, at:at + 64],
                                                        col[:, C_SGUB + g:C_SGUB + g + 1], z[:, Z_U + at:Z_U + at + 64],
                                                        ALU.add, ALU.mult), v_emptied if g == 3 else vector_step)
                    consume(1)
                    normalise("mla")
                    weighed("mla")
                    own.link(V.tensor_copy(signal[:, 1:2], sumsq[:, 0:1]), mix_done)
                    dve.wait_ge(squared, squares_by(10))
                    mean("mixed", 0, 4, sumsq[:, 4:8], 64, vector_step)
                    mean("mixed", 4, 3, sumsq[:, 8:11], GROUP, ms_ready)
                    consume(1)
                    wait_rstd("mixed")
                    a = mix[:, 0:GROUP].rearrange("p (h e) -> p h e", h=HEADS)
                    own.link(V.tensor_tensor(a, a, bc(stat("mixed", 0, 4), 2, 64), ALU.mult), vector_step)
                    b = mix[:, GROUP:D].rearrange("p (h e) -> p h e", h=3)
                    own.link(V.tensor_tensor(b, b, bc(stat("mixed", 4, 3), 2, GROUP), ALU.mult), mix_ready)
                    consume(1)
                    for c in range(2):
                        if c:
                            consume(1)
                        bank = take("proj", c)
                        part = x[:, t, c * CH:(c + 1) * CH]
                        own.link(V.tensor_tensor(part, part, bank[:, :], ALU.add), v_emptied)
                    own.link(V.tensor_copy(signal[:, 2:3], sumsq[:, 0:1]), x_ready)
                    dve.wait_ge(squared, squares_by(11))
                    dve.wait_ge(ffn_loaded, 16)
                    mean("ffn", 0, 1, sumsq[:, 11:12], D, ms_ready)
                    consume(1)
                    wait_rstd("ffn")
                    own.link(V.scalar_tensor_tensor(wide[:, t, :], x[:, t, :], stat("ffn"), ffn_gain, ALU.mult, ALU.mult), h2_ready)
                    consume(2)

                    def top16(chains):
                        for step_ in range(5):
                            r = step_ // 3
                            for vals, numbers, src in chains:
                                part = slice(8 * r, 8 * r + 8)
                                if step_ in (0, 3):
                                    ins = V.max(vals[:, part], src)
                                elif step_ in (1, 4):
                                    ins = V.max_index(numbers[:, part], vals[:, part], src)
                                else:
                                    ins = V.match_replace(src, vals[:, 0:8], src, LOWEST)
                                own.go(ins, vector_step)
                                dve.wait_ge(vector_step, own.value[id(vector_step)] - (len(chains) - 1))
                        dve.wait_ge(vector_step, own.value[id(vector_step)])

                    tv = top_v.rearrange("p (h c) k -> p h c k", c=2)
                    tf = top_f.rearrange("p (h c) k -> p h c k", c=2)
                    for part in range(2):
                        interleave = look_ahead if part else consume
                        h0 = part * (PH // 2)
                        hs = slice(h0, h0 + PH // 2)
                        dve.wait_ge(s_emptied, S_AT["keys", 2 * part + 1] + 1)
                        for j in range(2):
                            top16([(top_v[:, i, :], top_i[:, i, :], key_scores[:, i, :]) for i in range(2 * h0 + 4 * j, 2 * h0 + 4 * j + 4)])
                            interleave(1)
                        own.link(V.tensor_copy(top_f[:, 2 * h0:2 * h0 + PH, :], top_i[:, 2 * h0:2 * h0 + PH, :]), vector_step)
                        own.link(V.tensor_tensor(pairs[:, :, 0:2, :], tv[:, hs, 0, 0:1].unsqueeze(3).to_broadcast([P, PH // 2, 2, HALF_K]),
                                                 tv[:, hs, 1, :].rearrange("p h (r j) -> p h r j", j=HALF_K), ALU.add), vector_step)
                        own.link(V.tensor_tensor(pairs[:, :, 2:PAIR_ROWS, :], bc(tv[:, hs, 0, 1:TOPK], 3, HALF_K),
                                                 bc(tv[:, hs, 1, 0:HALF_K], 2, TOPK - 1), ALU.add), vector_step)
                        for j in range(2):
                            top16([(best[:, h0 + h, :], pos[:, h0 + h, :], pairs[:, h, :, :].rearrange("p r j -> p (r j)"))
                                   for h in range(2 * j, 2 * j + 2)])
                            interleave(1)
                        hi, hi_f, lo, lo_f = pos_hi[:, hs, :], pos_hi_f[:, hs, :], pos[:, hs, :], pos_f[:, hs, :]
                        second = expert_f[:, 0:PICKS // 2].rearrange("p (h k) -> p h k", k=TOPK)
                        own.go(V.tensor_scalar(hi, lo, 3, None, ALU.logical_shift_right), vector_step)
                        own.link(V.tensor_scalar(lo, lo, HALF_K - 1, None, ALU.bitwise_and), vector_step)
                        own.go(V.tensor_copy(hi_f, hi), vector_step)
                        own.link(V.tensor_copy(lo_f, lo), vector_step)
                        own.link(V.tensor_scalar(second, hi_f, 1.0, float(HALF_K), ALU.is_equal, ALU.mult), vector_step)
                        own.go(V.tensor_scalar(hi_f, hi_f, -1.0, 0.0, ALU.add, ALU.max), vector_step)
                        own.link(V.tensor_tensor(lo_f, lo_f, second, ALU.add), vector_step)
                        hk = onehot.rearrange("p h k i -> p (h k) i")
                        n = PICKS // 2
                        for c, which in enumerate((pos_hi_f, pos_f)):
                            w = which[:, hs, :].rearrange("p h k -> p (h k)")
                            own.link(V.tensor_tensor(hk, bc(iota16[:, :], 1, n), bc(w, 2, TOPK), ALU.is_equal), vector_step)
                            own.link(V.tensor_tensor(onehot, onehot, bc(tf[:, hs, c, :], 2, TOPK), ALU.mult), vector_step)
                            own.link(V.tensor_reduce(key_of[:, c, hs, :].rearrange("p h k -> p (h k)"), hk, AX, ALU.add), vector_step)
                            if not c:
                                interleave(1)
                        picks = slice(part * n, part * n + n)
                        k0 = key_of[:, 0, hs, :].rearrange("p h k -> p (h k)")
                        k1 = key_of[:, 1, hs, :].rearrange("p h k -> p (h k)")
                        own.link(V.scalar_tensor_tensor(expert_f[:, picks], k0, float(NKEY), k1, ALU.mult, ALU.add), vector_step)
                        own.link(V.tensor_scalar(expert[:, t, picks], expert_f[:, picks], lay[:, 2:3], None, ALU.add), experts_ready)
                        if not part:
                            if gat:
                                consume(LATE + ROUNDS - consumed[0])
                            look_ahead(2)
                            add_pe_sums()
                    own.link(V.tensor_tensor(gate[:, t, :, :], best, best[:, :, 0:1].to_broadcast([P, PH, TOPK]), ALU.subtract), shifted)
                    look_ahead(AHEAD - ahead[0])

                def gpsimd_program(pool):
                    own = Counted(pool)
                    G = nc.gpsimd
                    if gat:
                        G.sem_inc(pe_slots_free, NPE)
                    issued = [1]
                    copied = [0]

                    def fetch(g, b, n, tile, table):
                        G.sem_inc(gather_turn, 1)
                        G.tensor_copy(index_slot[:, b:b + 1], expert[:, tile, bass.ds(g * SLOTS + b, 1)]).then_inc(index_copied, 1)
                        pool.wait_ge(index_copied, n + 1)
                        G.sem_inc(gather_turn, 1)
                        G.indirect_dma_start(gathered[:, b, :], None, table,
                                             bass.IndirectOffsetOnAxis(ap=index_slot[:, b:b + 1], axis=0)).then_inc(row_loaded[b], 16)

                    def late_dots_round(g, slots=range(SLOTS)):
                        for b in slots:
                            pool.wait_ge(slots_free, g * SLOTS + (b + 1 - (AHEAD + 1) * SLOTS))
                            fetch(g, b, g * SLOTS + (b - (AHEAD + 1) * SLOTS), gt, experts_u)

                    def sums_round(g):
                        for b in range(SLOTS):
                            if b in DVE_SLOTS:
                                pool.wait_ge(slots_free, g * NDVE + (LATE_DOTS - NDVE + DVE_SLOTS.index(b) + 1))
                            else:
                                pool.wait_ge(slots_free, LATE_DOTS - SLOTS + b + 1)
                                pool.wait_ge(pe_slots_free, g * NPE + (PE_SLOTS.index(b) + 1))
                            fetch(g, b, g * SLOTS + (b + (LATE - 1) * SLOTS), gt, experts_v)

                    def issue_until(last):
                        if not gat:
                            return
                        first = issued[0]
                        issued[0] = last
                        if first < LATE:
                            rounds(pool, first + AHEAD, min(last, LATE) - first, late_dots_round)
                        if last > LATE:
                            start = max(first, LATE)
                            rounds(pool, start - LATE, last - start, sums_round)

                    if not pre:
                        def final_power(tile):
                            pool.wait_ge(ms_ready, tile + 1)
                            own.link(G.tensor_tensor(rstd[:, tile:tile + 1], ms[:, tile:tile + 1], half_neg[:, 0:1], ALU.pow), rstd_ready)

                        issue_until(2)
                        for tile in range(T - 1):
                            final_power(tile)
                        issue_until(LATE + ROUNDS)
                        final_power(T - 1)
                        return

                    def issue_ahead():
                        before = (LATE - 1 + ROUNDS) * SLOTS if gat else 0
                        used = ALL_SUMS if gat else 0

                        def ahead_round(g):
                            for b in range(SLOTS):
                                pool.wait_ge(slots_free, g * SLOTS + (used - SLOTS + b + 1))
                                fetch(g, b, g * SLOTS + (before + b), t, experts_u)

                        if both:
                            pool.wait_ge(s_filled, S_AT["next z", NW - 1] + 1)
                        pool.wait_ge(experts_ready, 1)
                        for b in range(SLOTS):
                            if gat and b in DVE_SLOTS:
                                pool.wait_ge(slots_free, ALL_SUMS - NDVE + DVE_SLOTS.index(b) + 1)
                            elif gat and b != PE_SLOTS[-1]:
                                pool.wait_ge(pe_slots_free, ROUNDS * NPE + PE_SLOTS.index(b) + 1)
                            elif gat:
                                pool.wait_ge(pe_summed, 2)
                            fetch(0, b, before + b, t, experts_u)
                        rounds(pool, 1, AHEAD - 1, ahead_round)
                        pool.wait_ge(experts_ready, 2)
                        rounds(pool, AHEAD, 1, ahead_round)

                    def power(name):
                        first, n = POWERS[name]
                        pool.wait_ge(ms_ready, power_at(name) + 1)
                        own.link(G.tensor_tensor(rstd[:, first:first + n], ms[:, first:first + n], half_neg[:, 0:n], ALU.pow), rstd_ready)

                    def rotate(view, n, half, at, done):
                        cos = bc(rope_sb[:, 0, t, at:at + half], 1, n)
                        sin = bc(rope_sb[:, 1, t, at:at + half], 1, n)
                        low, high = view[:, :, 0:half], view[:, :, half:2 * half]
                        part = [rot[:, i, 0:n * half].rearrange("p (n e) -> p n e", n=n) for i in range(4)]
                        own.go(G.tensor_tensor(part[0], low, cos, ALU.mult), gpsimd_step)
                        own.go(G.tensor_tensor(part[1], high, sin, ALU.mult), gpsimd_step)
                        own.go(G.tensor_tensor(part[2], high, cos, ALU.mult), gpsimd_step)
                        own.link(G.tensor_tensor(part[3], low, sin, ALU.mult), gpsimd_step)
                        own.go(G.tensor_tensor(low, part[0], part[1], ALU.subtract), gpsimd_step)
                        own.link(G.tensor_tensor(high, part[2], part[3], ALU.add), done)
                        pool.wait_ge(gpsimd_step, own.value[id(gpsimd_step)])

                    if gat:
                        late_dots_round(AHEAD + 1, range(FIRST_ROWS))
                    if not z_kept:
                        power("mix_in")
                    if gat:
                        late_dots_round(AHEAD + 1, range(FIRST_ROWS, SLOTS))
                        issued[0] = 2
                    if not gat:
                        pool.wait_ge(const_loaded, 3 * 16)
                    if t == 0:
                        pool.wait_ge(small_loaded, 7 * 16)
                        own.link(G.tensor_tensor(sgu_sb[:, :, :], sgu_sb[:, :, :], bc(tri_sb[:, :], 1, 4), ALU.mult), sgu_masked)
                    wait_z(pool, z_chunk(Z_AV))
                    rotate(z[:, 0:512].rearrange("p (n e) -> p n e", e=32), 16, 4, 0, rotated["diff"])
                    issue_until(4)
                    power("latent")
                    rotate(z[:, Z_KPE:Z_KPE + 32].rearrange("p (n e) -> p n e", n=1), 1, 16, 12, gpsimd_step)
                    issue_until(7)
                    if both:
                        pool.wait_ge(next_ms, 1)
                        own.link(G.tensor_tensor(rstd[:, NEXT:NEXT + 1], ms[:, NEXT:NEXT + 1], half_neg[:, 0:1], ALU.pow), next_rstd)
                    power("gate")
                    pool.wait_ge(s_emptied, S_AT["mq",] + 1)
                    rotate(mq[:, :, 64:MQ], HEADS, 16, 12, gpsimd_step)
                    pool.wait_ge(mk_ready, 1)
                    own.link(G.tensor_copy(mk[:, :, 64:MQ], bc(z[:, Z_KPE:Z_KPE + 32], 1, HEADS)), rotated["mla"])
                    issue_until(8)
                    wait_z(pool, NW - 1)
                    rotate(z[:, Z_DQ:Z_DQ + 512].rearrange("p (n e) -> p n e", e=64), 8, 8, 4, rotated["dil"])
                    issue_until(13)
                    power("mixed")
                    issue_until(16)
                    power("ffn")
                    issue_until(LATE + ROUNDS)
                    issue_ahead()

                {"sync": sync_program, "scalar": scalar_program, "tensor": tensor_program,
                 "vector": vector_program, "gpsimd": gpsimd_program}[name](eng)
                if not pre:
                    return
                if name == "scalar":
                    eng.wait_ge(gates_exped, 1)
                elif name == "tensor":
                    eng.wait_ge(s_filled, len(S_JOBS))
                elif name == "vector":
                    eng.wait_ge(slots_free, (ALL_SUMS if gat else 0) + AHEAD * SLOTS)
                issuer[name].sem_inc(step_done[name], 1)
                for other in issuer:
                    if other != name:
                        eng.wait_ge(step_done[other], layer * T + (t + 1))

            return step

        with nc.Block() as block:
            @block.sync
            def _(sp):
                sp.dma_start(x[:, 0, :], x_in[0:P, :]).then_inc(x_loaded[0], 16)
                sp.dma_start(id_sb[:, :], identity).then_inc(id_loaded, 16)
                head_chunk(sp, 0, 0)

            @block.gpsimd
            def _(pool):
                nc.gpsimd.memset(zeros[:, :], 0.0).then_inc(const_made, 1)
                nc.gpsimd.memset(half_neg[:, :], -0.5).then_inc(const_made, 1)
                nc.gpsimd.iota(iota16_i[:, :], [[1, TOPK]], base=0, channel_multiplier=0).then_inc(const_made, 1)
                pool.wait_ge(const_made, 3)
                nc.gpsimd.tensor_copy(iota16[:, :], iota16_i[:, :]).then_inc(const_made, 1)
                pool.wait_ge(const_made, 4)

        even, odd = steps_with(0), steps_with(1)

        def all_steps(name, eng):
            even(name, eng, (0, 0), None, (0, 1))
            odd(name, eng, (0, 1), (0, 0), (1, 0))
            even(name, eng, (1, 0), (0, 1), (1, 1))
            if L > 2:
                with eng.Fori(1, L - 1) as layer:
                    odd(name, eng, (layer, 1), (layer, 0), (layer + 1, 0))
                    even(name, eng, (layer + 1, 0), (layer, 1), (layer + 1, 1))
            odd(name, eng, (L - 1, 1), (L - 1, 0), None)
            even(name, eng, None, (L - 1, 1), None)

        with nc.Block() as block:
            @block.sync
            def _(sp):
                all_steps("sync", sp)

            @block.scalar
            def _(act):
                all_steps("scalar", act)

            @block.tensor
            def _(pe):
                all_steps("tensor", pe)

            @block.vector
            def _(dve):
                all_steps("vector", dve)

            @block.gpsimd
            def _(pool):
                all_steps("gpsimd", pool)


def shape_constants(seq):
    P, T = 128, seq // 128
    q = np.arange(seq)[:, None]
    k = np.arange(256)[None, :]
    causal = np.where(k <= q, 0.0, -1e30).astype(np.float32)
    count = np.zeros((seq, 256))
    for window, dil in ((128, 1), (512, 4), (2048, 16)):
        d = q - k
        count += (d >= 0) & (d % dil == 0) & (d // dil <= window // dil)
    dilated = np.where(count > 0, np.log(np.maximum(count, 1)), -1e30).astype(np.float32)
    masks = np.stack([causal, dilated]).reshape(2, T, P, 256).transpose(2, 0, 1, 3)
    masks = np.concatenate([masks[:, :, t, 0:P * (t + 1)] for t in range(T)], 2)
    angles = []
    for n_rot in (8, 16, 32):
        inv = np.float32(500000.0) ** (-np.arange(n_rot // 2, dtype=np.float32) * np.float32(2.0 / n_rot))
        angles.append(np.arange(seq, dtype=np.float32)[:, None] * inv[None, :])
    angles = np.concatenate(angles, 1).astype(np.float32)
    rope = np.stack([np.cos(angles), np.sin(angles)]).reshape(2, T, P, 28).transpose(2, 0, 1, 3)
    return {
        "masks": np.ascontiguousarray(masks), "rope": np.ascontiguousarray(rope),
        "triangle": np.triu(np.ones((P, P), np.float32)), "identity": np.eye(P, dtype=np.float32),
    }


def kernel(x, w_in, w_out, norm_mix, norm_ffn, diff_lambda, diff_head_norm, mla_q_norm, mla_kv_norm,
           mla_w_uq, mla_w_ukv, mla_out_norm, sgu_v_norm, sgu_w, sgu_b, sgu_out_norm, dil_out_norm,
           peer_w_q, peer_sub_keys, peer_u, peer_v, final_norm):
    import concourse.bacc as _bacc
    from concourse.bass_utils import run_bass_kernel_spmd as _run

    A = np.asarray
    L, seq, D = w_in.shape[0], x.shape[1], x.shape[2]
    n_experts = peer_u.shape[1]

    def down(a):
        a = A(a)
        return a.reshape(L, -1, 128).transpose(0, 2, 1)

    lam_init = [0.8 - 0.6 * math.exp(-0.3 * l) for l in range(L)]
    layer_consts = np.array([[v, 1.0 - v, l * n_experts] for l, v in enumerate(lam_init)], np.float32)
    arrays = {
        "x_in": A(x).reshape(seq, D), "w_in": A(w_in), "w_out": A(w_out), "w_q": A(peer_w_q),
        "columns": np.concatenate([down(norm_mix), down(mla_q_norm), down(mla_kv_norm), down(diff_head_norm),
                                   down(mla_out_norm), down(sgu_out_norm), down(dil_out_norm),
                                   A(sgu_b).transpose(0, 2, 1)], 2),
        "rows": np.concatenate([A(sgu_v_norm), A(diff_lambda).reshape(L, -1)], 1),
        "ffn_gains": A(norm_ffn),
        "layer_consts": np.repeat(layer_consts[:, None, :], 128, 1),
        "w_uq": A(mla_w_uq), "w_ukv": A(mla_w_ukv),
        "sgu_wt": A(sgu_w).transpose(0, 3, 1, 2), "keys_t": A(peer_sub_keys).transpose(0, 1, 3, 2).reshape(L, 128, -1),
        "experts_u": A(peer_u).reshape(L * n_experts, D), "experts_v": A(peer_v).reshape(L * n_experts, D),
        "final_gain": A(final_norm),
    }
    arrays.update(shape_constants(seq))
    nc = _bacc.Bacc("TRN2", target_bir_lowering=False, num_devices=1)
    feeds, args = {}, []
    for name, a in arrays.items():
        a = np.ascontiguousarray(a)
        feeds[f"in_{name}"] = a
        args.append(nc.dram_tensor(f"in_{name}", a.shape, mybir.dt.from_np(a.dtype), kind="ExternalInput").ap())
    args.append(nc.dram_tensor("out_0", (seq, D), mybir.dt.float32, kind="ExternalOutput").ap())
    bass_hybrid_trunk_peer(nc, *args)
    r = _run(nc, [feeds], core_ids=[0])
    return r.results[0]["out_0"].reshape(1, seq, D)
```
